# Optimizing a Trainium2 kernel written in Bass

```python
import math
import jax, jax.numpy as jnp
from jax import lax
import numpy as np

D_MODEL = 1024
BATCH = 1
SEQ = 512
DEPTH = 1
DEC_BATCH = 8
DEC_SEQ = 16
PAST_LEN = 512

CHUNK = 64
Q_BLOCK = 128
HEAD_DIM = 64
A_HEADS = 8
A_KV_HEADS = 2
A_REP = A_HEADS // A_KV_HEADS
IDX_HEADS = 4
IDX_DIM = 64
TOPK_MAX = 256
B_HEADS = 8
N_BRANCH = 2
ROPE_THETA = 10000.0
N_EXPERTS = 16
N_GROUPS = 4
EXP_PER_GROUP = N_EXPERTS // N_GROUPS
TOP_K = 2
D_EXPERT = 512
RMS_EPS = 1e-6
A_WIDTH = A_HEADS * HEAD_DIM
B_WIDTH = B_HEADS * HEAD_DIM
IN_SIZES = (A_WIDTH, A_KV_HEADS * HEAD_DIM, A_KV_HEADS * HEAD_DIM, IDX_HEADS * IDX_DIM, IDX_DIM,
            IDX_HEADS, B_WIDTH, B_WIDTH, B_WIDTH, N_BRANCH * D_MODEL)
N_IN = sum(IN_SIZES)

kernel_name = "hybrid_dsa_stickbreak_moe_stream_step"

def rms_norm(x, g):
    xf = x.astype(jnp.float32)
    y = xf * lax.rsqrt(jnp.mean(xf * xf, axis=-1, keepdims=True) + RMS_EPS)
    return (y * g.astype(jnp.float32)).astype(x.dtype)

def rope(x, pos):
    d = x.shape[-1]
    inv_freq = ROPE_THETA ** (-jnp.arange(0, d, 2, dtype=jnp.float32) / d)
    ang = pos.astype(jnp.float32)[:, None] * inv_freq[None, :]
    cos = jnp.cos(ang)[:, None, :]
    sin = jnp.sin(ang)[:, None, :]
    xf = x.astype(jnp.float32)
    x1, x2 = xf[..., : d // 2], xf[..., d // 2:]
    return jnp.concatenate([x1 * cos - x2 * sin, x2 * cos + x1 * sin], axis=-1).astype(x.dtype)

def gather_rows(a, idx):
    return jax.vmap(lambda a_b, i_b: a_b[i_b])(a, idx)

def dsa_block(q, qi, wi, pos_q, k, v, ki, pos_k, n_sel):
    b, tq = q.shape[:2]
    dots = jnp.einsum("bqhd,bsd->bqhs", qi, ki).astype(jnp.float32) * (IDX_DIM ** -0.5)
    score = jnp.einsum("bqhs,bqh->bqs", jax.nn.relu(dots), wi.astype(jnp.float32))
    admissible = (pos_k[None, :] // CHUNK) <= (pos_q[:, None] // CHUNK)
    score = jnp.where(admissible[None], score, -jnp.inf)
    top_val, top_idx = lax.top_k(score, n_sel)
    valid = jnp.isfinite(top_val)
    k_sel = gather_rows(k, top_idx)
    v_sel = gather_rows(v, top_idx)
    qg = q.reshape(b, tq, A_KV_HEADS, A_REP, HEAD_DIM)
    logits = jnp.einsum("bqgrd,bqjgd->bqgrj", qg, k_sel).astype(jnp.float32) * (HEAD_DIM ** -0.5)
    logits = jnp.where(valid[:, :, None, None, :], logits, -jnp.inf)
    probs = jax.nn.softmax(logits, axis=-1).astype(v.dtype)
    out = jnp.einsum("bqgrj,bqjgd->bqgrd", probs, v_sel)
    return out.reshape(b, tq, A_HEADS, HEAD_DIM)

def stick_breaking_block(q, pos_q, k, v, pos_k):
    z = jnp.einsum("bqhd,bshd->bhqs", q, k).astype(jnp.float32) * (HEAD_DIM ** -0.5)
    earlier = pos_k[None, :] < pos_q[:, None]
    log_keep = jnp.where(earlier, jax.nn.log_sigmoid(-z), 0.0)
    between = lax.cumsum(log_keep, axis=3, reverse=True) - log_keep
    att = jnp.where(earlier, jnp.exp(jax.nn.log_sigmoid(z) + between), 0.0)
    return jnp.einsum("bhqs,bshd->bqhd", att.astype(v.dtype), v)

def blocked(fn, q_arrays, pos):
    b, t = q_arrays[0].shape[:2]
    nb = t // Q_BLOCK

    def split(a):
        return jnp.moveaxis(a.reshape((b, nb, Q_BLOCK) + a.shape[2:]), 1, 0)

    out = lax.map(lambda args: fn(*args), tuple(split(a) for a in q_arrays) + (pos.reshape(nb, Q_BLOCK),))
    return jnp.moveaxis(out, 0, 1).reshape((b, t) + out.shape[3:])

def token_mixer(h, pos, past, w_in, qn_g, kn_g, w_branch_a, w_branch_b, w_out):
    b, t, _ = h.shape
    split_pts = [int(s) for s in np.cumsum(IN_SIZES)[:-1]]
    qa, ka, va, qi, ki, wi, qb, kb, vb, gl = jnp.split(h @ w_in, split_pts, axis=-1)
    qa = rope(rms_norm(qa.reshape(b, t, A_HEADS, HEAD_DIM), qn_g), pos)
    ka = rope(rms_norm(ka.reshape(b, t, A_KV_HEADS, HEAD_DIM), kn_g), pos)
    va = va.reshape(b, t, A_KV_HEADS, HEAD_DIM)
    qi = rope(qi.reshape(b, t, IDX_HEADS, IDX_DIM), pos)
    ki = rope(ki[:, :, None, :], pos)[:, :, 0, :]
    wi = wi * (IDX_HEADS ** -0.5)
    qb = qb.reshape(b, t, B_HEADS, HEAD_DIM)
    kb = kb.reshape(b, t, B_HEADS, HEAD_DIM)
    vb = vb.reshape(b, t, B_HEADS, HEAD_DIM)
    new_rows = (ka, va, ki, kb, vb)
    if past is None:
        keys = new_rows
        pos_k = pos
    else:
        keys = tuple(jnp.concatenate([p_, n_], axis=1) for p_, n_ in zip(past, new_rows))
        pos_k = jnp.arange(keys[0].shape[1], dtype=jnp.int32)
    k_a, v_a, k_i, k_b, v_b = keys
    n_sel = min(TOPK_MAX, k_a.shape[1] // 4)

    def mix_a(q_, qi_, wi_, pq):
        return dsa_block(q_, qi_, wi_, pq, k_a, v_a, k_i, pos_k, n_sel)

    def mix_b(q_, pq):
        return stick_breaking_block(q_, pq, k_b, v_b, pos_k)

    if past is None:
        o_a = blocked(mix_a, (qa, qi, wi), pos)
        o_b = blocked(mix_b, (qb,), pos)
    else:
        o_a = mix_a(qa, qi, wi, pos)
        o_b = mix_b(qb, pos)
    gates = jax.nn.sigmoid(gl.astype(jnp.float32)).astype(h.dtype).reshape(b, t, N_BRANCH, D_MODEL)
    merged = (gates[:, :, 0] * (o_a.reshape(b, t, A_WIDTH) @ w_branch_a)
              + gates[:, :, 1] * (o_b.reshape(b, t, B_WIDTH) @ w_branch_b))
    return merged @ w_out, new_rows

def grouped_moe(h, w_router, b_router, w_gate, w_up, w_down):
    b, t, d = h.shape
    hf = h.reshape(b * t, d)
    affinity = jax.nn.softmax((hf @ w_router).astype(jnp.float32), axis=-1)
    biased = affinity + b_router.astype(jnp.float32)
    group_score = lax.top_k(biased.reshape(-1, N_GROUPS, EXP_PER_GROUP), TOP_K)[0].sum(-1)
    best_group = jnp.argmax(group_score, axis=-1)
    in_group = (jnp.arange(N_EXPERTS) // EXP_PER_GROUP)[None, :] == best_group[:, None]
    _, top_idx = lax.top_k(jnp.where(in_group, biased, -jnp.inf), TOP_K)
    top_w = jnp.take_along_axis(affinity, top_idx, axis=-1)
    top_w = top_w / jnp.sum(top_w, axis=-1, keepdims=True)
    gates = jnp.sum(jax.nn.one_hot(top_idx, N_EXPERTS, dtype=jnp.float32) * top_w[..., None], axis=1)
    gates = gates.astype(h.dtype)
    y = jnp.zeros_like(hf)
    for e in range(N_EXPERTS):
        hidden = jax.nn.silu(hf @ w_gate[e]) * (hf @ w_up[e])
        y = y + gates[:, e:e + 1] * (hidden @ w_down[e])
    return y.reshape(b, t, d)

def trunk_layer(x, c, pos, past, p):
    mod = jax.nn.silu(c) @ p["w_ada"] + p["b_ada"]
    sh1, sc1, g1, sh2, sc2, g2 = [m[:, None, :] for m in jnp.split(mod, 6, axis=-1)]
    h = rms_norm(x, p["norm1_g"]) * (1 + sc1) + sh1
    mix, rows = token_mixer(h, pos, past, p["w_in"], p["qn_g"], p["kn_g"],
                            p["w_branch_a"], p["w_branch_b"], p["w_out"])
    x = x + g1 * mix
    h = rms_norm(x, p["norm2_g"]) * (1 + sc2) + sh2
    x = x + g2 * grouped_moe(h, p["w_router"], p["b_router"], p["w_exp_gate"], p["w_exp_up"], p["w_exp_down"])
    return x, rows

def setup_inputs(seed: int = 0) -> dict:
    key = jax.random.key(seed)
    ks = jax.random.split(key, 24)

    def nrm(k, shape, scale):
        return jax.random.normal(k, shape, jnp.float32) * scale

    return {
        "x_prompt": nrm(ks[0], (BATCH, SEQ, D_MODEL), 1.0),
        "x_sample": nrm(ks[1], (DEC_BATCH, DEC_SEQ, D_MODEL), 1.0),
        "cache_a_k": nrm(ks[2], (DEPTH, DEC_BATCH, PAST_LEN, A_KV_HEADS, HEAD_DIM), 1.0),
        "cache_a_v": nrm(ks[3], (DEPTH, DEC_BATCH, PAST_LEN, A_KV_HEADS, HEAD_DIM), 1.0),
        "cache_idx_k": nrm(ks[4], (DEPTH, DEC_BATCH, PAST_LEN, IDX_DIM), 1.0),
        "cache_b_k": nrm(ks[5], (DEPTH, DEC_BATCH, PAST_LEN, B_HEADS, HEAD_DIM), 1.0),
        "cache_b_v": nrm(ks[6], (DEPTH, DEC_BATCH, PAST_LEN, B_HEADS, HEAD_DIM), 1.0),
        "c_prompt": nrm(ks[7], (BATCH, D_MODEL), 1.0),
        "c_sample": nrm(ks[8], (DEC_BATCH, D_MODEL), 1.0),
        "norm1_g": 1.0 + nrm(ks[9], (DEPTH, D_MODEL), 0.02),
        "norm2_g": 1.0 + nrm(ks[10], (DEPTH, D_MODEL), 0.02),
        "w_ada": nrm(ks[11], (DEPTH, D_MODEL, 6 * D_MODEL), 0.5 * D_MODEL ** -0.5),
        "b_ada": nrm(ks[12], (DEPTH, 6 * D_MODEL), 0.01),
        "w_in": nrm(ks[13], (DEPTH, D_MODEL, N_IN), D_MODEL ** -0.5),
        "qn_g": 1.0 + nrm(ks[14], (DEPTH, HEAD_DIM), 0.02),
        "kn_g": 1.0 + nrm(ks[15], (DEPTH, HEAD_DIM), 0.02),
        "w_branch_a": nrm(ks[16], (DEPTH, A_WIDTH, D_MODEL), A_WIDTH ** -0.5),
        "w_branch_b": nrm(ks[17], (DEPTH, B_WIDTH, D_MODEL), B_WIDTH ** -0.5),
        "w_out": nrm(ks[18], (DEPTH, D_MODEL, D_MODEL), D_MODEL ** -0.5),
        "w_router": nrm(ks[19], (D_MODEL, N_EXPERTS), D_MODEL ** -0.5),
        "b_router": nrm(ks[20], (N_EXPERTS,), 0.01),
        "w_exp_gate": nrm(ks[21], (DEPTH, N_EXPERTS, D_MODEL, D_EXPERT), D_MODEL ** -0.5),
        "w_exp_up": nrm(ks[22], (DEPTH, N_EXPERTS, D_MODEL, D_EXPERT), D_MODEL ** -0.5),
        "w_exp_down": nrm(ks[23], (DEPTH, N_EXPERTS, D_EXPERT, D_MODEL), D_EXPERT ** -0.5),
    }

def reference(x_prompt, x_sample, cache_a_k, cache_a_v, cache_idx_k, cache_b_k, cache_b_v,
              c_prompt, c_sample, norm1_g, norm2_g, w_ada, b_ada, w_in, qn_g, kn_g,
              w_branch_a, w_branch_b, w_out, w_router, b_router, w_exp_gate, w_exp_up, w_exp_down):
    pos_p = jnp.arange(x_prompt.shape[1], dtype=jnp.int32)
    past_len = cache_a_k.shape[2]
    pos_s = past_len + jnp.arange(x_sample.shape[1], dtype=jnp.int32)
    xp, xs = x_prompt, x_sample
    rows_p, rows_s = [], []
    for l in range(DEPTH):
        p = {
            "norm1_g": norm1_g[l], "norm2_g": norm2_g[l], "w_ada": w_ada[l], "b_ada": b_ada[l],
            "w_in": w_in[l], "qn_g": qn_g[l], "kn_g": kn_g[l],
            "w_branch_a": w_branch_a[l], "w_branch_b": w_branch_b[l], "w_out": w_out[l],
            "w_router": w_router, "b_router": b_router,
            "w_exp_gate": w_exp_gate[l], "w_exp_up": w_exp_up[l], "w_exp_down": w_exp_down[l],
        }
        xp, rp = trunk_layer(xp, c_prompt, pos_p, None, p)
        past = (cache_a_k[l], cache_a_v[l], cache_idx_k[l], cache_b_k[l], cache_b_v[l])
        xs, rs = trunk_layer(xs, c_sample, pos_s, past, p)
        rows_p.append(rp)
        rows_s.append(rs)

    def stack(rows, i):
        return jnp.stack([r[i] for r in rows], axis=0)

    new_a_k_p, new_a_v_p, new_idx_k_p = stack(rows_p, 0), stack(rows_p, 1), stack(rows_p, 2)
    new_b_k_p, new_b_v_p = stack(rows_p, 3), stack(rows_p, 4)
    new_a_k_s, new_a_v_s, new_idx_k_s = stack(rows_s, 0), stack(rows_s, 1), stack(rows_s, 2)
    new_b_k_s, new_b_v_s = stack(rows_s, 3), stack(rows_s, 4)
    return (xp, xs, new_a_k_p, new_a_v_p, new_idx_k_p, new_b_k_p, new_b_v_p,
            new_a_k_s, new_a_v_s, new_idx_k_s, new_b_k_s, new_b_v_s)


_drawn_inputs = setup_inputs


def setup_inputs(seed=0):
    import zlib

    import numpy as np

    out = dict(_drawn_inputs(seed))
    spreads = {}
    factors = {'norm1_g': 2.948, 'qn_g': 8.0, 'kn_g': 3.014}
    for name, (base, spread) in spreads.items():
        noise = np.random.default_rng([zlib.crc32(name.encode()), seed]).standard_normal(out[name].shape)
        drawn = base * np.exp(spread * noise) if base else spread * noise
        out[name] = __import__('jax').numpy.asarray(drawn.astype(out[name].dtype))
    for name, factor in factors.items():
        out[name] = (out[name] * factor).astype(out[name].dtype)
    return out
```

```python
from contextlib import ExitStack

import numpy as np

import concourse.bass as bass
from concourse import mybir

F32 = mybir.dt.float32
BF16 = mybir.dt.bfloat16
I32 = mybir.dt.int32
U32 = mybir.dt.uint32
ALU = mybir.AluOpType
ACT = mybir.ActivationFunctionType
X = mybir.AxisListType.X

P = 128
D = 1024
KD = D // P
SEQ = 512
DEC_B, DEC_S, PAST = 8, 16, 512
NT = SEQ // P + DEC_B * DEC_S // P
TOK = NT * P
SMP = NT - 1
HD = 64
AH, AKV, REP = 8, 2, 4
IH = 4
BH = 8
NPAIR = BH // 2
NE, NG, EPG = 16, 4, 4
DE = 512
CHUNK = 64
TOPK_P = min(256, SEQ // 4)
TOPK_S = min(256, (PAST + DEC_S) // 4)
EPS = 1e-6
ROPE_THETA = 10000.0
NC_KEYS = PAST // P
SKEYS = PAST + P
SPAD = -TOPK_S % 8
BIG = 1e30
OUT_OF_REACH = -3.0e38
TAKEN = -3.39e38
TAKEN_BELOW = -3.2e38
COL = dict(qa=0, kvq=512, kiwi=1024, qb=1092, kb=1604, vb=2116, gl=2628)
JOBS = 26
PAIRS = JOBS // 2
NCOND = 1 + DEC_B

SLAB = 4096
NSLAB = 4
O_F = NSLAB * SLAB
O_QB = O_F + 5120
O_KB = O_QB + 2560
O_VB = O_KB + 2560
O_VA = O_VB + 2560
O_OA = O_VA + 640
O_OB = O_OA + 2560
O_H = O_OB + 2560
O_CF = O_H + 5120
NCF = 4 * 128 + 16 + 16 + JOBS + 2
O_CB = O_CF + NCF
NCB = 5 * 128 + 2 * 8 * 128
O_MB = O_CB + NCB // 2
O_ST = O_MB + 960
O_TMP = O_ST + 400
N_TMP = 9830
MEM = O_TMP + N_TMP


def host_constants():
    i = np.arange(P)
    ident = np.eye(P, dtype=np.float32)
    neg_tri = -(i[:, None] >= i[None, :]).astype(np.float32)
    neg_ones = -np.ones((P, P), np.float32)
    own = (i[:, None] // DEC_S) == (i[None, :] // DEC_S)
    own_batch = np.where(own, 0.0, OUT_OF_REACH).astype(np.float32)
    cf = np.zeros((P, NCF), np.float32)
    cf[:, 0:512] = np.concatenate([ident, neg_tri, neg_ones, own_batch], 1)
    cf[:, 512:528] = np.arange(16)
    cf[:, 528:544] = np.arange(16) // EPG
    cf[:, 544:544 + JOBS] = np.arange(JOBS)
    cf[:, 544 + JOBS] = EPS
    cb = np.zeros((P, NCB), np.float32)
    cb[:, 0:128] = ident
    cb[:, 128:256] = np.where(i[:, None] < i[None, :], 0.0, -BIG)
    cb[:, 256:384] = np.where((i[None, :] // CHUNK) <= (i[:, None] // CHUNK), 0.0, -BIG)
    cb[:, 384:512] = (i[:, None] < i[None, :])
    cb[:, 512:640] = 1.0
    for b in range(DEC_B):
        row = np.arange(P) % DEC_S
        cb[:, 640 + 128 * b:768 + 128 * b] = i[:, None] == (DEC_S * b + row)[None, :]
        ok = (i[:, None] // DEC_S == b) & (i[:, None] % DEC_S < row[None, :])
        cb[:, 1664 + 128 * b:1792 + 128 * b] = np.where(ok, 0.0, -BIG)
    pos = np.concatenate([np.arange(SEQ), np.tile(PAST + np.arange(DEC_S), DEC_B)]).astype(np.float32)
    inv = (np.float32(ROPE_THETA) ** (-np.arange(0, HD, 2, dtype=np.float32) / np.float32(HD))).astype(np.float32)
    ang = pos[:, None] * inv[None, :]
    cos, sin = np.cos(ang).astype(np.float32), np.sin(ang).astype(np.float32)
    rot = np.concatenate([cos, cos, -sin, sin], 1).reshape(NT, P, 128).transpose(1, 0, 2)
    token = np.arange(TOK, dtype=np.int32).reshape(NT, P).T
    slot = np.arange(JOBS * P, dtype=np.int32)
    return {
        "const_f": cf,
        "const_b": (cb.view(np.uint32) >> 16).astype(np.uint16).view(np.float32),
        "rotary": np.ascontiguousarray(rot),
        "token_ids": np.stack([np.broadcast_to(token[:, :, None], (P, NT, 2)),
                               2 * token[:, :, None] + np.arange(2, dtype=np.int32)], -1),
        "empty_slots": np.stack([0 * slot, 2 * TOK + slot], -1),
    }


def build(nc, a, o, scratch):
    ctx = ExitStack()
    with ctx:
        def sem(name):
            return ctx.enter_context(nc.semaphore(name))

        mem = ctx.enter_context(nc.sbuf_tensor("mem", [P, MEM], F32))
        ps = ctx.enter_context(nc.psum_tensor("ps", [P, 8 * 512], F32))

        def view(at, n, pat=None, **dims):
            v = mem[:, at:at + n]
            return v if pat is None else v.rearrange(pat, **dims)

        def bview(at, n, pat=None, **dims):
            v = mem[:, at:at + n // 2].bitcast(BF16)
            return v if pat is None else v.rearrange(pat, **dims)

        slabs = []
        slabs += [("ada", i) for i in range(8)]
        slabs += [("in", "qa"), ("in", "kvq"), ("in", "kiwi"), ("in", "qb"), ("in", "vb"), ("idx",), ("in", "kb")]
        slabs += [("ada", i) for i in range(8, 12)]
        slabs += [("ak",), ("av",)] + [("b", b) for b in range(DEC_B)]
        slabs += [("gl", 0, 0), ("gl", 1, 0), ("bra",), ("brb",), ("wo", 0), ("wo", 1)]
        slab_no = {s: n for n, s in enumerate(slabs)}

        slab = [view(SLAB * i, SLAB) for i in range(NSLAB)]
        slab_k = [s.rearrange("p (k n) -> p k n", k=KD) for s in slab]
        slab_4 = [s.rearrange("p (k n) -> p k n", k=4) for s in slab]
        featT = view(O_F, 5120, "p (j t) -> p j t", j=8)
        xt = view(O_F, 5120, "p (t n) -> p t n", t=NT)
        mergedT = view(O_F, 5120, "p (j t) -> p j t", j=8)
        qbT = view(O_QB, 2560, "p (j t) -> p j t", j=NPAIR)
        kbT = view(O_KB, 2560, "p (j t) -> p j t", j=NPAIR)
        vb = view(O_VB, 2560, "p (t n) -> p t n", t=NT)
        va = view(O_VA, 640, "p (t n) -> p t n", t=NT)
        oaT = view(O_OA, 2560, "p (j t) -> p j t", j=REP)
        obT = view(O_OB, 2560, "p (j t) -> p j t", j=NPAIR)
        hT = view(O_H, 5120, "p (j t) -> p j t", j=KD)
        gx = [view(O_QB + SLAB * i, SLAB, "p (k n) -> p k n", k=KD) for i in range(2)]
        assert O_QB + 2 * SLAB <= O_OA
        x1 = view(O_H, 5120, "p (t n) -> p t n", t=NT)
        ident = view(O_CF, 128)
        neg_tri = view(O_CF + 128, 128)
        neg_ones = view(O_CF + 256, 128)
        own_batch = view(O_CF + 384, 128)
        iota_e = view(O_CF + 512, 16)
        group_e = view(O_CF + 528, 16)
        iota_j = view(O_CF + 544, JOBS)
        eps = view(O_CF + 544 + JOBS, 1)
        ident_b = bview(O_CB, 128)
        later_b = bview(O_CB + 64, 128)
        chunk_b = bview(O_CB + 128, 128)
        before_b = bview(O_CB + 192, 128)
        ones_b = bview(O_CB + 256, 128)
        pick_b = bview(O_CB + 320, 1024, "p (b n) -> p b n", b=DEC_B)
        newmask_b = bview(O_CB + 832, 1024, "p (b n) -> p b n", b=DEC_B)
        mb_at = {1: 0, 2: 128, 3: 320, 4: 576}
        mask_bias = {q: bview(O_MB + mb_at[q], P * (q + 1)) for q in (1, 2, 3)}
        mask_bias[SMP] = bview(O_MB + mb_at[4], SKEYS)
        s9T = view(O_ST, KD * NCOND, "p (k n) -> p k n", k=KD)
        st = O_ST + KD * NCOND
        ssum = view(st, NT); rstd = view(st + 5, NT)
        ss10 = view(st + 10, 50, "p (t n) -> p t n", t=NT); rr10 = view(st + 60, 50, "p (t n) -> p t n", t=NT)
        wis = view(st + 110, 20, "p (t n) -> p t n", t=NT)
        nmax = view(st + 130, 4); rsum = view(st + 134, 4); rrec = view(st + 138, 4)
        top8 = view(st + 142, 8)
        ssum2 = view(st + 150, NT); rstd2 = view(st + 155, NT)
        tokid = view(st + 160, 4 * NT, "p (t i a) -> p t i a", t=NT, i=2).bitcast(I32)
        rot = view(O_OA, 640, "p (t n) -> p t n", t=NT)
        gains = view(O_OA + 640, 640, "p (h d) -> p h d", d=HD)
        b9 = [view(O_OA + 1280 + 512 * i, 512)[0:NCOND] for i in range(2)]
        g9 = [view(O_OA + 2304 + 512 * i, 512)[0:NCOND] for i in range(2)]
        m9 = [view(O_OA + 3328 + 512 * i, 512)[0:NCOND] for i in range(2)]
        ht = [view(O_TMP + 1024 * i, 1024) for i in range(2)]
        bc1 = {False: view(O_TMP + 2048, 2048), True: view(O_TMP + 4096, 2048)}
        c9 = view(O_TMP + 6144, 1024)[0:NCOND]
        s9 = view(O_TMP + 7168, 1024)[0:NCOND]
        NTK = 15 * HD + IH
        tok = view(O_TMP, 5 * NTK, "p (t n) -> p t n", t=NT)
        t0 = O_TMP + 5 * NTK
        ro = [view(t0 + 1024 * i, 1024) for i in range(2)]
        swp = view(t0 + 2048, 960)
        sqb = view(t0 + 3008, 640)
        kbt = [view(O_OA + 512 * i, 512) for i in range(2)]
        sc_at = {1: 0, 2: 256, 3: 640, 4: 1152}
        score = {q: view(O_TMP + sc_at[q], P * (q + 1)) for q in (1, 2, 3)}
        score[SMP] = view(O_TMP + sc_at[4], SKEYS + SPAD)
        O_IX = O_TMP + 1152 + SKEYS + SPAD
        idxT = view(O_IX, 2048, "p (j s) -> p j s", j=4)
        qi_bd = view(O_IX + 2048, 512, "p (h j c) -> p h j c", h=IH, j=4)
        relu = [view(O_IX + 2560 + 2560 * i, 2560, "p (h s) -> p h s", h=IH) for i in range(2)]
        assert O_IX + 2560 + 5120 <= MEM
        prob = [view(O_TMP + 640 * i, 640) for i in range(3)]
        probT = [view(O_TMP + 1920 + 640 * i, 640, "p (c q) -> p c q", q=P) for i in range(2)]
        kaT = view(O_IX + 2560, 4096, "p (b s) -> p b s", b=DEC_B)
        qa_bd = view(O_IX + 2560 + 4096, 1024, "p (b n) -> p b n", b=DEC_B)
        ebuf = [view(O_TMP + 1280 * i, 1280) for i in range(2)]
        att = [view(O_TMP + 2560 + 1280 * i, 1280) for i in range(2)]
        kcT = [view(O_F + 2048 * i, 2048, "p (j s) -> p j s", j=NPAIR) for i in range(2)]
        qb_bd = view(O_F + 4096, 1024, "p (b j c) -> p b j c", b=DEC_B, j=NPAIR)
        g1 = {False: view(O_TMP, 1024), True: view(O_TMP + 1024, 1024)}
        bc2 = {False: view(O_TMP + 2048, 2048), True: view(O_TMP + 4096, 2048)}
        g2 = {False: view(O_TMP + 2048, 1024), True: view(O_TMP + 3072, 1024)}
        gated = [view(O_TMP + 6144 + 512 * i, 512) for i in range(2)]
        sg = [[view(O_TMP + 7168 + 640 * i + 320 * j, 320) for j in range(2)] for i in range(2)]
        gb = [[view(O_TMP + 8448 + 640 * i + 320 * j, 320) for j in range(2)] for i in range(2)]
        h2 = [view(O_TMP + 7168 + 1024 * i, 1024) for i in range(2)]
        wr = view(O_OB, 128, "p (k n) -> p k n", k=KD)
        sq_junk = view(O_OB + 128, 1024)
        h2T = [view(24576 + 1024 * i, 1024, "p (k t) -> p k t", k=KD) for i in range(2)]
        rt = O_TMP + 4096
        R3 = {}
        for n, name in enumerate("lg aff bi ing bm oh1 oh2 pr sb t1 t2".split()):
            R3[name] = view(rt + 80 * n, 80, "p (t e) -> p t e", t=NT)
        R3["lg"] = view(O_OB + 1152, 80, "p (t e) -> p t e", t=NT)
        rt += 880
        R4 = {}
        for n, name in enumerate("p q r s m1 u v m2".split()):
            R4[name] = view(rt + 20 * n, 20, "p (t g) -> p t g", t=NT)
        rt += 160
        gpad = view(rt, 40, "p (t g) -> p t g", t=NT)
        v8 = view(rt + 40, 40, "p (t g) -> p t g", t=NT)
        i8 = view(rt + 80, 40, "p (t g) -> p t g", t=NT).bitcast(U32)
        v8b = view(rt + 120, 40, "p (t g) -> p t g", t=NT)
        i8b = view(rt + 160, 40, "p (t g) -> p t g", t=NT).bitcast(U32)
        rt += 200
        gidx = view(rt, 5); eidx = view(rt + 5, 10, "p (t i) -> p t i", t=NT)
        rmx = view(rt + 15, 5); rsm = view(rt + 20, 5); rrc = view(rt + 25, 5)
        aw = [view(rt + 30 + 5 * i, 5) for i in range(2)]
        den = view(rt + 40, 5); rden = view(rt + 45, 5)
        ew = [view(rt + 50 + 5 * i, 5) for i in range(2)]
        slotf = view(rt + 60, 10, "p (t i) -> p t i", t=NT)
        slots = view(rt + 70, 10, "p (t i) -> p t i", t=NT).bitcast(U32)
        cnt = view(rt + 80, 16); nt = [view(rt + 96 + 16 * i, 16) for i in range(2)]
        ends = [view(rt + 128 + 16 * i, 16) for i in range(2)]; base = view(rt + 160, 16)
        ejf = view(rt + 176, JOBS); eji = view(rt + 202, JOBS).bitcast(I32)
        prf = view(rt + 228, PAIRS); prs = view(rt + 241, 1); pri = view(rt + 242, 1).bitcast(I32)
        idj = [view(rt + 244 + i, 1).bitcast(U32) for i in range(2)]
        idd = [view(rt + 246 + i, 1).bitcast(U32) for i in range(2)]
        brb = view(rt + 274, 16)
        sel_b = bview(rt + 290, 80, "p (t e) -> p t e", t=NT)
        cmp = view(rt + 330, JOBS * NE, "p (j e) -> p j e", j=JOBS)
        ids = view(rt + 330 + JOBS * NE, 2 * (JOBS + 2), "p (j a) -> p j a", a=2).bitcast(U32)
        assert rt + 330 + JOBS * NE + 2 * (JOBS + 2) <= O_TMP + 6144
        mw_at = [n % NSLAB for n in (slab_no[("bra",)], slab_no[("brb",)], slab_no[("wo", 0)], slab_no[("wo", 1)])] + [4, 5]
        mw = [view(i * SLAB, SLAB) for i in mw_at]
        o_x = 24576
        hx = [view(o_x + 1024 * i, 1024) for i in range(2)]
        hxT = [view(o_x + 2048 + 1024 * i, 1024, "p (k t) -> p k t", k=KD) for i in range(2)]
        sil = [view(o_x + 4096 + 512 * i, 512) for i in range(2)]
        hid = [view(o_x + 5120 + 512 * i, 512) for i in range(2)]
        hidT = [view(o_x + 6144 + 512 * i, 512, "p (k t) -> p k t", k=4) for i in range(2)]
        yj = [view(o_x + 7168 + 1024 * i, 1024) for i in range(2)]
        assert o_x + 9216 <= O_H
        y2 = [view(2048 * t, 2048, "p (i n) -> p i n", i=2) for t in range(NT)]
        yc = [view(2048 * NT + 1024 * t, 1024) for t in range(NT)]

        def bank(i, n=512):
            return ps[:, 512 * i:512 * i + n]

        xp = a["x_prompt"].rearrange("b s d -> (b s) d")
        xs = a["x_sample"].rearrange("b s d -> (b s) d")
        w_in, w_ada = a["w_in"][0], a["w_ada"][0]
        modd, h2d, yd, slot_tok = scratch
        rows2 = {n: (o[i].rearrange("l b s h d -> (l b s) (h d)"), o[j].rearrange("l b s h d -> (l b s) (h d)"))
                 for n, i, j in (("ak", 2, 7), ("av", 3, 8), ("bk", 5, 10), ("bv", 6, 11))}
        rows2["ix"] = (o[4].rearrange("l b s d -> (l b s) d"), o[9].rearrange("l b s d -> (l b s) d"))
        rows2["y"] = (o[0].rearrange("b s d -> (b s) d"), o[1].rearrange("b s d -> (b s) d"))

        def out_rows(name, t):
            p_, s_ = rows2[name]
            return s_[0:P, :] if t == SMP else p_[P * t:P * (t + 1), :]

        def by_k(w, c, n, k=KD):
            return w[:, c:c + n].rearrange("(k p) n -> p k n", k=k)

        def slab_moves(s, n):
            f, k8, k4 = slab[n % NSLAB], slab_k[n % NSLAB], slab_4[n % NSLAB]
            if s[0] == "ada":
                return [(k8, by_k(w_ada, 512 * s[1], 512))]
            if s[0] == "in":
                w = 68 if s[1] == "kiwi" else 512
                return [(k8[:, :, 0:w], by_k(w_in, COL[s[1]], w))]
            if s[0] == "gl":
                return [(k8, by_k(w_in, COL["gl"] + D * s[1] + 512 * s[2], 512))]
            if s[0] == "bra":
                w = a["w_branch_a"][0].rearrange("(g r d) n -> g d r n", g=AKV, r=REP)
                return [(k4[HD * g:HD * g + HD], w[g]) for g in range(AKV)]
            if s[0] == "brb":
                return [(k4, by_k(a["w_branch_b"][0], 0, D, 4))]
            if s[0] == "wo":
                return [(k8, by_k(a["w_out"][0], 512 * s[1], 512))]
            if s[0] == "idx":
                v = f[:, 0:2048].rearrange("p (j c n) -> p j c n", j=4, c=4)
                return [(v[:, b // 2, :, HD * (b % 2):HD * (b % 2) + HD],
                         a["cache_idx_k"][0, b].rearrange("(c p) d -> p c d", p=P)) for b in range(DEC_B)]
            if s[0] in ("ak", "av"):
                v = f.rearrange("p (b c n) -> p b c n", b=DEC_B, c=4)
                src = a["cache_a_k" if s[0] == "ak" else "cache_a_v"][0].rearrange("b (c p) h d -> b p c (h d)", p=P)
                return [(v[:, b], src[b]) for b in range(DEC_B)]
            v = f.rearrange("p (w c n) -> p w c n", w=2, c=4)
            return [(v[:, w], a[n_][0, s[1]].rearrange("(c p) h d -> p c (h d)", p=P))
                    for w, n_ in enumerate(("cache_b_k", "cache_b_v"))]

        slab_ld = [sem(f"slab_loaded{i}") for i in range(NSLAB)]
        slab_used = sem("slab_used")
        landed, total = [], [0] * NSLAB
        for n, s in enumerate(slabs):
            total[n % NSLAB] += 16 * len(slab_moves(s, n))
            landed.append(total[n % NSLAB])

        place, used, nfull, used_full = {}, [0] * 8, {}, [0] * 8

        def plan(key, slot, own_signal=False):
            place[key] = (slot, used[slot])
            used[slot] += 1
            if not own_signal:
                used_full[slot] += 1
                nfull[key] = used_full[slot]

        turn = [0]

        def plan_next(key):
            plan(key, turn[0] % 8)
            turn[0] += 1

        A_UNITS = [("p", q, r, g) for q in range(SMP) for r in range(REP) for g in range(AKV)] + \
                  [("s", b) for b in range(DEC_B)]
        NA = len(A_UNITS)
        NP_A = SMP * AH

        def a_group(u):
            return u // AH if u < NP_A else SMP + (u - NP_A)

        NB = BH + DEC_B
        marks = {}
        plan_next("s9T")
        for i in range(8):
            plan_next(("ada", i))
        for t in range(NT):
            for h in range(2):
                plan_next(("h1T", t, h))
        for s in ("qa", "kvq", "kiwi"):
            for t in range(NT):
                plan_next((s, t))
        for m in range(4):
            for h in range(2):
                plan_next(("qb", m, h))
        for t in range(NT):
            plan_next(("vb", t))
        for t in range(NT):
            for h in range(2):
                plan_next(("roT", t, h))
        for j in range(4):
            plan_next(("idxT", j))
        for h in range(IH):
            plan_next(("sdot", h))
        for par in range(2):
            plan_next(("sdotn", par))
        for q in (3, 2, 1):
            for h in range(IH):
                plan_next(("dot", q, h))
        for t in range(NT):
            plan_next(("kb", t))
            if t:
                plan_next(("kbT", t - 1))
        plan_next(("kbT", NT - 1))
        for i in range(8, 12):
            plan_next(("ada", i))
        marks["a"] = list(used)
        for b in range(DEC_B):
            plan(("kaT", b), b)
        for u in range(NA + 3):
            if u < NA:
                plan(("L", u), (0, 1, 2)[u % 3] if u < NP_A else (0, 2)[u % 2])
            if 2 <= u < NA + 2:
                plan(("T", u - 2), 4 + u % 2 if u - 2 < NP_A else 4)
            if u >= 3 and (u - 3 == 0 or a_group(u - 3) != a_group(u - 4)):
                plan(("O", a_group(u - 3)), 6 + a_group(u - 3) % 2, own_signal=True)
        marks["b"] = list(used)
        for i in range(NB):
            if i >= BH:
                for j in range(NPAIR):
                    plan(("kcT", i, j), 2 if j % 2 == 0 else 5)
        for i in range(NB):
            if i >= BH or i % 2 == 0:
                g = i // 2 if i < BH else 4 + i - BH
                plan(("bO", g), 6 + g % 2, own_signal=True)
        marks["m"] = list(used)
        for i in range(16):
            for j in range(4):
                plan(("mg", i, j), 4 * (i % 2) + j)
        marks["o"] = list(used)
        for t in range(NT):
            for n in range(2):
                plan(("wo", t, n), (2 * t + n) % 4)
        for t in range(NT):
            for h in range(2):
                plan(("h2T", t, h), 4 + h)
            plan(("lg", t), 6)
        plan("pre", 7)
        plan("cnt", 0)
        marks["e"] = list(used)

        full = [sem(f"psum_full{i}") for i in range(8)]
        free = [sem(f"psum_free{i}") for i in range(8)]

        def may_fill(key):
            s, k = place[key]
            if k:
                nc.tensor.wait_ge(free[s], k)
            return bank(s)

        def filled(key, ins):
            ins.then_inc(full[place[key][0]], 1)

        def result(eng, key):
            eng.wait_ge(full[place[key][0]], nfull[key])
            return bank(place[key][0])

        def was_read(eng, key):
            eng.wait_ge(free[place[key][0]], place[key][1] + 1)

        def read(key, ins):
            ins.then_inc(free[place[key][0]], 1)

        (c_ld, x_ld, c9_ld, bg_ld0, bg_ld1, m9_st0, m9_st1, bc1_ld, rot_ld, rows_st, kb_st0, kb_st1, bc2_ld,
         x1_ld, wr_ld, h2_st0, h2_st1, g2_ld, zero_st, scat, out_st,
         ro_st0, ro_st1) = (
            sem(n) for n in "c_ld x_ld c9_ld bg_ld0 bg_ld1 m9_st0 m9_st1 bc1_ld rot_ld rows_st kb_st0 kb_st1 bc2_ld "
                            "x1_ld wr_ld h2_st0 h2_st1 g2_ld zero_st scat out_st "
                            "ro_st0 ro_st1".split())
        bg_ld, m9_st, kb_st, h2_st = ((bg_ld0, bg_ld1), (m9_st0, m9_st1), (kb_st0, kb_st1),
                                      (h2_st0, h2_st1))
        ro_st = (ro_st0, ro_st1)
        act_did, dve_did, pool_did = sem("act_did"), sem("dve_did"), sem("pool_did")
        (s9_ready, s9T_ready, m9_raw, m9_ready, h_sums, h_ready, sq_ready, ss10_ready,
         rms10_ready, ro_ready, qibd_ready, relu_used, kbt_ready, vb_ready, mask_ready) = (
            sem(n) for n in "s9_ready s9T_ready m9_raw m9_ready h_sums h_ready sq_ready ss10_ready "
                            "rms10_ready ro_ready qibd_ready relu_used "
                            " kbt_ready vb_ready mask_ready".split())
        (qabd_ready, nmax_ready, exp_ready, prob_ready, pT_act, pT_dve, av_done) = (
            sem(n) for n in " qabd_ready nmax_ready exp_ready prob_ready pT_act pT_dve av_done".split())
        (qbbd_ready, z_full, l_ready, sp_ready, cum_full, att_ready, kcT_act, kcT_dve, bv_done) = (
            sem(n) for n in "qbbd_ready z_full l_ready sp_ready cum_full att_ready kcT_act kcT_dve bv_done".split())
        (sg_ready, gb_ready, merged, merge_read, x1_ready, sum2_ready, h2_ready, h2T_ready, e_in, e_out,
         sel_ready, jobs_ready, slots_ready, wo_done) = (
            sem(n) for n in "sg_ready gb_ready merged merge_read x1_ready sum2_ready h2_ready h2T_ready e_in "
                            "e_out sel_ready jobs_ready slots_ready wo_done".split())
        gx_ld = [sem(f"gate_half_loaded{g}") for g in range(2)]
        mw_ld = [sem(f"mw_ld{i}") for i in range(6)]
        mw_free = [sem(f"mw_free{i}") for i in range(6)]
        (idj_ready, hx_ld, hx_free, xT_full, xT_act, xT_dve, gate_full, up_full, sil_done, hid_done, hT_full,
         hidT_done, down_full, y_act, y_dve, y_st) = (
            [sem(f"{n}{i}") for i in range(2)] for n in
            "idj_ready hx_ld hx_free xT_full xT_act xT_dve gate_full up_full sil_done hid_done hidT_full "
            "hidT_done down_full y_act y_dve y_st".split())
        held = {e: sem(f"held_{e}") for e in ("act", "dve", "pe", "pool")}
        a_half, y_all = sem("a_half"), sem("y_all")
        y_ld = [sem(f"y_loaded{t}") for t in range(NT)]

        class Own:

            def __init__(self, eng, s):
                self.eng, self.s, self.n = eng, s, 0

            def __call__(self, ins):
                self.n += 1
                ins.then_inc(self.s, 1)

            def settle(self):
                self.eng.wait_ge(self.s, self.n)

        def bcast(v, shape, axis):
            return v.unsqueeze(axis).broadcast_to(shape)

        def bo_group(i):
            return i // 2 if i < BH else 4 + i - BH

        zcol = {0: 0, 1: 512, 3: 896, 2: 1024}

        block = ctx.enter_context(nc.Block())

        @block.sync
        def _(sp):
            sp.dma_start(view(O_CF, NCF), a["const_f"]).then_inc(c_ld, 16)
            sp.dma_start(view(O_CB, NCB // 2), a["const_b"]).then_inc(c_ld, 16)
            for n, s in enumerate(slabs):
                if n >= NSLAB:
                    sp.wait_ge(slab_used, n - NSLAB + 1)
                for dst, src in slab_moves(s, n):
                    sp.dma_start(dst, src).then_inc(slab_ld[n % NSLAB], 16)
                if n == NSLAB:
                    sp.dma_start(slot_tok, a["empty_slots"]).then_inc(zero_st, 16)
                if s == ("brb",):
                    sp.wait_ge(bv_done, NB)
                    sp.wait_ge(rows_st, 160)
                    for g in range(2):
                        sp.dma_start(gx[g], by_k(w_in, COL["gl"] + D * g + 512, 512)).then_inc(gx_ld[g], 16)

            def expert_part(k, e):
                w = k % 3
                src = a[("w_exp_gate", "w_exp_up", "w_exp_down")[w]][0, e].rearrange("a (k p) n -> p (a k) n", p=P)
                sp.dma_start(mw[k].rearrange("p (k n) -> p k n", k=4 if w == 2 else KD), src).then_inc(mw_ld[k], 16)

            sp.wait_ge(merge_read, 1)
            for k in range(3):
                if k == 2:
                    sp.wait_ge(wo_done, 1)
                expert_part(k, slice(0, 1))
            sp.wait_ge(jobs_ready, 1)
            for p in range(2):
                sp.wait_ge(y_st[p], 16)
            e = nc.sync.value_load(eji[0:1, 1:2], min_val=0, max_val=NE - 1)
            for k in range(3, 6):
                expert_part(k, bass.ds(e, 1))
            pairs = nc.sync.value_load(pri[0:1, 0:1], min_val=NE // 2, max_val=PAIRS)
            with sp.Fori(1, pairs) as i:
                for p in range(2):
                    e = nc.sync.value_load(eji[0:1, bass.ds(2 * i + p, 1)], min_val=0, max_val=NE - 1)
                    for k in range(3 * p, 3 * p + 3):
                        sp.wait_ge(mw_free[k], i)
                        expert_part(k, bass.ds(e, 1))
            sp.wait_ge(y_all, 1)
            for t in range(NT):
                sp.dma_start(y2[t], yd[2 * P * t:2 * P * t + 2 * P, :].rearrange("(p i) n -> p i n", i=2)).then_inc(y_ld[t], 16)
            for t in range(NT):
                sp.wait_ge(e_out, 100 + t + 1)
                sp.dma_start(out_rows("y", t), yc[t]).then_inc(out_st, 16)
            sp.wait_ge(out_st, 16 * NT)

        @block.gpsimd
        def _(pool):
            own = Own(pool, pool_did)
            g = nc.gpsimd
            pool.dma_start(rot, a["rotary"]).then_inc(rot_ld, 16)
            for i, n in enumerate(("qn_g", "kn_g")):
                lo, hi = (0, AH) if i == 0 else (AH, AH + AKV)
                for h in range(lo, hi):
                    pool.dma_start(gains[:, h, :], a[n].broadcast_to([P, HD])).then_inc(rot_ld, 16)
            pool.dma_start(tokid, a["token_ids"]).then_inc(rot_ld, 16)
            nstore = [0, 0]

            def ada(i):
                b = i % 2
                scale_part = i // 2 in (1, 4)
                if i >= 2:
                    pool.wait_ge(m9_ready, i - 1)
                pool.dma_start(b9[b], a["b_ada"][0:1, 512 * i:512 * i + 512].broadcast_to([NCOND, 512])).then_inc(bg_ld[b], 16)
                gsrc = a["norm1_g" if i < 6 else "norm2_g"][0:1, 512 * (i % 2):512 * (i % 2) + 512]
                pool.dma_start(g9[b], gsrc.broadcast_to([NCOND, 512])).then_inc(bg_ld[b], 16)
                pool.wait_ge(m9_raw, i + 1)
                pool.wait_ge(bg_ld[b], 32 * (i // 2 + 1))
                if not scale_part:
                    g.tensor_tensor(m9[b], m9[b], b9[b], ALU.add).then_inc(m9_ready, 1)
                else:
                    own(g.tensor_tensor(m9[b], m9[b], b9[b], ALU.add))
                    own.settle()
                    own(g.tensor_scalar(m9[b], m9[b], 1.0, None, ALU.add))
                    own.settle()
                    g.tensor_tensor(m9[b], m9[b], g9[b], ALU.mult).then_inc(m9_ready, 1)
                pool.wait_ge(m9_ready, i + 1)
                pool.dma_start(modd[:, 512 * i:512 * i + 512], m9[b]).then_inc(m9_st[b], 16)

            def spread(dst, lo, n, s):
                pool.dma_start(dst[False], modd[0:1, lo:lo + n].broadcast_to([P, n])).then_inc(s, 16)
                for b in range(DEC_B):
                    pool.dma_start(dst[True][DEC_S * b:DEC_S * b + DEC_S, :],
                                   modd[1 + b:2 + b, lo:lo + n].broadcast_to([DEC_S, n])).then_inc(s, 16)

            for i in range(4):
                ada(i)
            pool.wait_ge(m9_st[0], 32)
            pool.wait_ge(m9_st[1], 32)
            spread(bc1, 0, 2048, bc1_ld)
            for i in range(4, 8):
                ada(i)
            for t in range(NT):
                pool.wait_ge(ro_ready, t + 1)
                rs_ = ro[t % 2]
                pool.dma_start(out_rows("ak", t), rs_[:, 512:640]).then_inc(ro_st[t % 2], 16)
                pool.dma_start(out_rows("ix", t), rs_[:, 896:960]).then_inc(ro_st[t % 2], 16)
                pool.dma_start(out_rows("av", t), va[:, t, :]).then_inc(rows_st, 16)
            for t in range(NT):
                pool.wait_ge(vb_ready, t + 1)
                pool.dma_start(out_rows("bv", t), vb[:, t, :]).then_inc(rows_st, 16)
            for t in range(NT):
                pool.wait_ge(kbt_ready, t + 1)
                pool.dma_start(out_rows("bk", t), kbt[t % 2]).then_inc(kb_st[t % 2], 16)
            for i in range(8, 12):
                ada(i)
            pool.wait_ge(m9_st[0], 96)
            pool.wait_ge(m9_st[1], 96)
            pool.wait_ge(bv_done, NB)
            spread(g1, 2048, 1024, bc2_ld)
            spread(bc2, 3072, 2048, bc2_ld)
            for i in range(16):
                m, h = i // 2, i % 2
                pool.wait_ge(gb_ready, i + 1)
                g.tensor_tensor(mergedT[:, m, 320 * h:320 * h + 320], gb[i % 2][0], gb[i % 2][1],
                                ALU.add).then_inc(merged, 1)
            pool.wait_ge(merge_read, 1)
            pool.dma_start(x1[:, 0:SMP, :], xp.rearrange("(t p) n -> p t n", p=P)).then_inc(x1_ld, 16)
            pool.dma_start(x1[:, SMP, :], xs).then_inc(x1_ld, 16)
            pool.dma_start(wr, a["w_router"].rearrange("(k p) n -> p k n", k=KD)).then_inc(wr_ld, 16)
            for t in range(NT):
                pool.wait_ge(h2_ready, t + 1)
                pool.dma_start(h2d[P * t:P * t + P, :], h2[t % 2]).then_inc(h2_st[t % 2], 16)
            pool.wait_ge(h2_ready, NT)
            spread(g2, 5120, 1024, g2_ld)
            pool.dma_start(brb, a["b_router"].unsqueeze(0).broadcast_to([P, NE])).then_inc(g2_ld, 16)
            pool.wait_ge(zero_st, 16)
            pool.wait_ge(rot_ld, 16 * 12)
            pool.wait_ge(slots_ready, 1)
            for t in range(NT):
                for i in range(2):
                    pool.indirect_dma_start(slot_tok, bass.IndirectOffsetOnAxis(ap=slots[:, t, i:i + 1], axis=0),
                                            tokid[:, t, i, :], None).then_inc(scat, 16)
            pool.wait_ge(scat, 160)
            for p in range(2):
                pool.dma_start(ids[:, p:JOBS:2, :], slot_tok.rearrange("(j p) a -> p j a", p=P).bitcast(U32)[:, p:JOBS:2, :],
                               allow_slow_non_contiguous=True).then_inc(y_st[p], 16)
            pool.wait_ge(h2_st[0], 48)
            pool.wait_ge(h2_st[1], 32)
            pool.wait_ge(jobs_ready, 1)

            def hold(sm, v):
                pool.wait_ge(sm, v)
                pool.sem_inc(held["pool"], 1)

            for p in range(2):
                pool.wait_ge(y_st[p], 16)
            for p in range(2):
                pool.indirect_dma_start(hx[p], None, h2d,
                                        bass.IndirectOffsetOnAxis(ap=ids[:, p, 0:1], axis=0)).then_inc(hx_ld[p], 16)
            pairs = g.value_load(pri[0:1, 0:1], min_val=NE // 2, max_val=PAIRS)
            with pool.Fori(0, pairs) as i:
                for p in range(2):
                    hold(hx_free[p], i + 1)
                    hold(idj_ready[p], i + 1)
                    pool.indirect_dma_start(hx[p], None, h2d,
                                            bass.IndirectOffsetOnAxis(ap=idj[p], axis=0)).then_inc(hx_ld[p], 16)
                for p in range(2):
                    hold(y_act[p], i + 2)
                    hold(y_dve[p], 2 * i + 3)
                    pool.indirect_dma_start(yd, bass.IndirectOffsetOnAxis(ap=idd[p], axis=0),
                                            yj[p], None).then_inc(y_st[p], 16)
            for p in range(2):
                hold(y_st[p], pairs * 16 + 16)
                hold(hx_ld[p], pairs * 16 + 16)
            pool.sem_inc(y_all, 1)
            pool.wait_ge(rows_st, 160)
            pool.wait_ge(ro_st[0], 96)
            pool.wait_ge(ro_st[1], 64)
            pool.wait_ge(kb_st[0], 48)
            pool.wait_ge(kb_st[1], 32)

        @block.scalar
        def _(act):
            own = Own(act, act_did)
            s = nc.scalar

            def copy_out(key, dst, src=None, scale=1.0):
                r = result(act, key)
                ins = s.activation(dst, r if src is None else src, ACT.Copy, scale=scale)
                return ins

            act.dma_start(c9[0:1, :], a["c_prompt"]).then_inc(c9_ld, 16)
            act.dma_start(c9[1:NCOND, :], a["c_sample"]).then_inc(c9_ld, 16)
            act.dma_start(xt[:, 0:SMP, :], xp.rearrange("(t p) n -> p t n", p=P)).then_inc(x_ld, 16)
            act.dma_start(xt[:, SMP, :], xs).then_inc(x_ld, 16)
            act.wait_ge(c9_ld, 32)
            s.activation(s9, c9, ACT.Silu).then_inc(s9_ready, 1)
            act.wait_ge(x_ld, 32)
            act.wait_ge(c_ld, 32)
            for t in range(NT):
                own(s.activation(ht[t % 2], xt[:, t, :], ACT.Square, accum_out=ssum[:, t:t + 1]))
                own.settle()
            s.activation(rstd, ssum, ACT.Sqrt, scale=1.0 / D, bias=eps).then_inc(h_sums, 1)

            def ada(i):
                if i >= 2:
                    act.wait_ge(m9_st[i % 2], 16 * (i // 2))
                r = result(act, ("ada", i))
                own(s.activation(m9[i % 2], r[0:NCOND], ACT.Copy))
                own.settle()
                act.sem_inc(m9_raw, 1)
                act.sem_inc(free[place[("ada", i)][0]], 1)

            for i in range(8):
                ada(i)

            for t in range(NT):
                for h in range(2):
                    r = result(act, ("h1T", t, h))
                    read(("h1T", t, h), s.activation(hT[:, 4 * h:4 * h + 4, P * t:P * t + P],
                                                     r.rearrange("p (k q) -> p k q", k=4), ACT.Copy))
            for t in range(NT):
                r = result(act, ("qa", t))
                read(("qa", t), s.activation(tok[:, t, 0:512], r, ACT.Copy))
            for t in range(NT):
                r = result(act, ("kvq", t))
                own(s.activation(tok[:, t, 512:640], r[:, 0:128], ACT.Copy))
                own(s.activation(va[:, t, :], r[:, 128:256], ACT.Copy))
                read(("kvq", t), s.activation(tok[:, t, 640:896], r[:, 256:512], ACT.Copy))
            for t in range(NT):
                r = result(act, ("kiwi", t))
                was_read(act, ("kvq", t))
                read(("kiwi", t), s.activation(tok[:, t, 896:964], r[:, 0:68], ACT.Copy))
                was_read(act, ("kiwi", t))
                own.settle()
                if t:
                    act.wait_ge(ss10_ready, t)
                s.activation(sqb, tok[:, t, 0:640], ACT.Square).then_inc(sq_ready, 1)
            for m in range(4):
                for h in range(2):
                    r = result(act, ("qb", m, h))
                    read(("qb", m, h), s.activation(qbT[:, m, 320 * h:320 * h + 320], r[:, 0:320], ACT.Copy,
                                                    scale=HD ** -0.5))
            act.wait_ge(ss10_ready, NT)
            s.activation(rr10, ss10, ACT.Sqrt, scale=1.0 / HD, bias=eps).then_inc(rms10_ready, 1)
            for t in range(NT):
                r = result(act, ("vb", t))
                own(s.activation(vb[:, t, :], r, ACT.Copy))
                own.settle()
                act.sem_inc(vb_ready, 1)
                act.sem_inc(free[place[("vb", t)][0]], 1)
            for t in range(NT):
                for h in range(2):
                    r = result(act, ("roT", t, h))
                    read(("roT", t, h), s.activation(featT[:, 4 * h:4 * h + 4, P * t:P * t + P],
                                                     r.rearrange("p (k q) -> p k q", k=4), ACT.Copy))
            for j in range(4):
                r = result(act, ("idxT", j))
                read(("idxT", j), s.activation(idxT[:, j, :], r, ACT.Copy))
            act.wait_ge(ro_st[0], 96)
            act.wait_ge(ro_st[1], 64)
            for h in range(IH):
                r = result(act, ("sdot", h))
                read(("sdot", h), s.activation(relu[0][:, h, 0:PAST], r, ACT.Relu))
            for par in range(2):
                r = result(act, ("sdotn", par))[:, 0:2 * P].rearrange("p (h s) -> p h s", h=2)
                dst = relu[0].rearrange("p (h e) s -> p h e s", e=2)[:, :, par, PAST:SKEYS]
                read(("sdotn", par), s.activation(dst, r, ACT.Relu))
            for n, q in enumerate((3, 2, 1)):
                if n >= 1:
                    act.wait_ge(relu_used, n)
                for h in range(IH):
                    r = result(act, ("dot", q, h))
                    read(("dot", q, h), s.activation(relu[(n + 1) % 2][:, h, 0:P * (q + 1)], r[:, 0:P * (q + 1)], ACT.Relu))
            for t in range(NT + 1):
                if t < NT:
                    r = result(act, ("kb", t))
                    if t >= 2:
                        act.wait_ge(kb_st[t % 2], 16 * (t // 2))
                    own(s.activation(kbt[t % 2], r, ACT.Copy))
                    own.settle()
                    act.sem_inc(kbt_ready, 1)
                    act.sem_inc(free[place[("kb", t)][0]], 1)
                if t >= 1:
                    r = result(act, ("kbT", t - 1))
                    read(("kbT", t - 1), s.activation(kbT[:, :, P * (t - 1):P * t],
                                                      r.rearrange("p (k q) -> p k q", k=NPAIR), ACT.Copy))
            for i in range(8, 12):
                ada(i)
            act.wait_ge(relu_used, 4)
            for b in range(DEC_B):
                r = result(act, ("kaT", b))
                read(("kaT", b), s.activation(kaT[:, b, :], r, ACT.Copy))

            def width(u):
                return P * (A_UNITS[u][1] + 1) if u < NP_A else SKEYS

            for i in range(NA + 2):
                if i < NA:
                    w = width(i)
                    sl, _k = place[("L", i)]
                    act.wait_ge(nmax_ready, i + 1)
                    if i >= 3:
                        result(act, ("T", i - 3))
                    own(s.activation(prob[i % 3][:, 0:w], ps[:, 512 * sl:512 * sl + w], ACT.Exp,
                                     bias=nmax[:, i % 4:i % 4 + 1], accum_out=rsum[:, i % 4:i % 4 + 1]))
                    own.settle()
                    act.sem_inc(exp_ready, 1)
                    act.sem_inc(free[sl], 1)
                if i >= 2 and i % 2 == 0:
                    u = i - 2
                    w = width(u)
                    sl, _k = place[("T", u)]
                    result(act, ("T", u))
                    if u >= 2:
                        act.wait_ge(av_done, u - 1)
                    own(s.activation(probT[u % 2].rearrange("p c q -> p (c q)")[:, 0:w],
                                     ps[:, 512 * sl:512 * sl + w], ACT.Copy))
                    own.settle()
                    act.sem_inc(pT_act, 1)
                    act.sem_inc(free[sl], 1)

            def wb(i):
                return 1280 if i < BH else SKEYS

            def b_exp(i):
                e = ebuf[i % 2][:, 0:wb(i)]
                act.wait_ge(z_full, i + 1)
                own(s.activation(e, ps[:, 1536 * (i % 2):1536 * (i % 2) + wb(i)], ACT.Abs))
                own.settle()
                own(s.activation(e, e, ACT.Exp, scale=-1.0))
                own.settle()
                s.activation(e, e, ACT.Ln, bias=1.0).then_inc(l_ready, 1)

            def b_att(i):
                act.wait_ge(cum_full, i + 1)
                if i >= 2:
                    act.wait_ge(bv_done, i - 1)
                base_ = 1536 * (i % 2)
                s.activation(att[i % 2][:, 0:wb(i)], ps[:, base_:base_ + wb(i)], ACT.Exp).then_inc(att_ready, 1)

            def b_keys(i):
                for j in (0, 2):
                    r = result(act, ("kcT", i, j))
                    s_, k_ = place[("kcT", i, j)]
                    own(s.activation(kcT[i % 2][:, j, :], r, ACT.Copy))
                    own.settle()
                    act.sem_inc(kcT_act, 1)
                    act.sem_inc(free[s_], 1)

            for i in range(NB + 1):
                if i == BH:
                    b_att(i - 1)
                    b_keys(i)
                if i < NB:
                    b_exp(i)
                if BH <= i < NB - 1:
                    b_keys(i + 1)
                if i >= 1 and i != BH:
                    b_att(i - 1)
            for i in range(16):
                if i >= 2:
                    act.wait_ge(gb_ready, i - 1)
                for j in range(2):
                    r = result(act, ("mg", i, j))
                    if i == 0 and j == 0:
                        act.wait_ge(bv_done, NB)
                    own(s.activation(sg[i % 2][j], r[:, 0:320], ACT.Sigmoid))
                    own.settle()
                    act.sem_inc(free[place[("mg", i, j)][0]], 1)
                act.sem_inc(sg_ready, 1)
            act.wait_ge(merge_read, 1)
            for t in range(NT + 2):
                if t < NT:
                    act.wait_ge(x1_ready, t + 1)
                    own(s.activation(sq_junk, x1[:, t, :], ACT.Square, accum_out=ssum2[:, t:t + 1]))
                    own.settle()
                    s.activation(rstd2[:, t:t + 1], ssum2[:, t:t + 1], ACT.Sqrt, scale=1.0 / D, bias=eps).then_inc(sum2_ready, 1)
                if t >= 2:
                    u = t - 2
                    if u >= 2:
                        result(act, ("lg", u - 2))
                    for h in range(2):
                        r = result(act, ("h2T", u, h))
                        own(s.activation(h2T[u % 2][:, 4 * h:4 * h + 4, :], r.rearrange("p (k q) -> p k q", k=4), ACT.Copy))
                        own.settle()
                        act.sem_inc(free[place[("h2T", u, h)][0]], 1)
                    act.sem_inc(h2T_ready, 1)
            act.wait_ge(e_in, 1)
            s.activation(R3["aff"], R3["lg"], ACT.Exp).then_inc(e_out, 100)
            for p in range(2):
                act.sem_inc(y_act[p], 1)
            act.wait_ge(jobs_ready, 1)
            act.wait_ge(xT_full[0], 1)
            act.sem_inc(hx_free[0], 1)
            s.activation(hxT[0][:, 0:4, :], bank(0).rearrange("p (k q) -> p k q", k=4), ACT.Copy).then_inc(xT_act[0], 1)
            pairs = s.value_load(pri[0:1, 0:1], min_val=NE // 2, max_val=PAIRS)
            with act.Fori(0, pairs) as i:
                def hold(sm, v):
                    act.wait_ge(sm, v)
                    act.sem_inc(held["act"], 1)

                def seen(sm, v, now_free):
                    act.wait_ge(sm, v)
                    act.sem_inc(now_free, 1)

                def turn_x(p, n):
                    seen(xT_full[p], n, hx_free[p])
                    s.activation(hxT[p][:, 0:4, :], bank(0).rearrange("p (k q) -> p k q", k=4), ACT.Copy).then_inc(xT_act[p], 1)

                def silu(p):
                    seen(gate_full[p], i + 1, mw_free[3 * p])
                    s.activation(sil[p], bank(2), ACT.Silu).then_inc(sil_done[p], 1)

                def down(p):
                    seen(down_full[p], i + 1, mw_free[3 * p + 2])
                    hold(y_st[p], i * 16 + 16)
                    s.activation(yj[p][:, 0:512], bank(5), ACT.Copy).then_inc(y_act[p], 1)

                silu(0)
                turn_x(1, i + 1)
                silu(1)
                down(0)
                turn_x(0, i + 2)
                down(1)
            for t in range(NT):
                act.wait_ge(y_ld[t], 16)
                s.activation(y2[t][:, 0, :], y2[t][:, 0, :], ACT.Copy, scale=ew[0][:, t:t + 1]).then_inc(a_half, 1)

        @block.vector
        def _(dve):
            own = Own(dve, dve_did)
            v = nc.vector

            def step(ins):
                own(ins)
                own.settle()

            r = result(dve, "s9T")
            own(v.tensor_copy(s9T, r[:, 0:KD * NCOND].rearrange("p (k n) -> p k n", k=KD)))
            own.settle()
            dve.sem_inc(s9T_ready, 1)
            dve.sem_inc(free[place["s9T"][0]], 1)
            dve.wait_ge(rot_ld, 16 * 12)
            step(v.tensor_scalar(gains[:, 0:AH, :], gains[:, 0:AH, :], HD ** -0.5, None, ALU.mult))
            dve.wait_ge(h_sums, 1)
            step(v.reciprocal(rstd, rstd))
            dve.wait_ge(bc1_ld, 16 * 9)
            for t in range(NT):
                m = bc1[t == SMP]
                if t >= 2:
                    result(dve, ("h1T", t - 2, 1))
                step(v.scalar_tensor_tensor(ht[t % 2], xt[:, t, :], rstd[:, t:t + 1], m[:, 1024:2048], ALU.mult, ALU.mult))
                v.tensor_tensor(ht[t % 2], ht[t % 2], m[:, 0:1024], ALU.add).then_inc(h_ready, 1)
            for t in range(NT):
                dve.wait_ge(sq_ready, t + 1)
                v.tensor_reduce(ss10[:, t, :], sqb.rearrange("p (h d) -> p h d", d=HD), X, ALU.add).then_inc(ss10_ready, 1)
            dve.wait_ge(rms10_ready, 1)
            step(v.reciprocal(rr10, rr10))
            for t in range(NT):
                x_ = tok[:, t, 0:960].rearrange("p (h d) -> p h d", d=HD)
                sw = swp.rearrange("p (h d) -> p h d", d=HD)
                half = HD // 2
                step(v.tensor_tensor(x_[:, 0:10, :], x_[:, 0:10, :], bcast(rr10[:, t, :], [P, 10, HD], 2), ALU.mult))
                step(v.tensor_tensor(x_[:, 0:10, :], x_[:, 0:10, :], gains, ALU.mult))
                sin = rot[:, t, 64:128]
                own(v.tensor_tensor(sw[:, :, 0:half], x_[:, :, half:HD], bcast(sin[:, 0:half], [P, 15, half], 1), ALU.mult))
                step(v.tensor_tensor(sw[:, :, half:HD], x_[:, :, 0:half], bcast(sin[:, half:HD], [P, 15, half], 1), ALU.mult))
                step(v.tensor_tensor(x_, x_, bcast(rot[:, t, 0:64], [P, 15, HD], 1), ALU.mult))
                if t >= 2:
                    result(dve, ("roT", t - 2, 1))
                    dve.wait_ge(ro_st[t % 2], 32 * (t // 2))
                own(v.tensor_tensor(ro[t % 2][:, 0:512].rearrange("p (r g d) -> p g r d", r=REP, g=AKV),
                                    tok[:, t, 0:512].rearrange("p (g r d) -> p g r d", r=REP, g=AKV),
                                    swp[:, 0:512].rearrange("p (g r d) -> p g r d", r=REP, g=AKV), ALU.add))
                own(v.tensor_tensor(ro[t % 2][:, 512:960], tok[:, t, 512:960], swp[:, 512:960], ALU.add))
                own(v.tensor_tensor(ro[t % 2][:, 960:1024], tok[:, t, 896:960], swp[:, 896:960], ALU.add))
                step(v.tensor_scalar(wis[:, t, :], tok[:, t, 960:964], IH ** -0.5 * HD ** -0.5, None, ALU.mult))
                dve.sem_inc(ro_ready, 1)
            own(v.memset(view(O_IX + 2048, 512), 0.0))
            own(v.memset(score[SMP][:, SKEYS:SKEYS + SPAD], 3.0e38))
            own.settle()
            was_read(dve, ("roT", SMP, 1))
            for h in range(IH):
                for par in range(2):
                    src = featT[HD * (h % 2):HD * (h % 2) + HD, 5 + h // 2, SEQ:TOK].rearrange(
                        "p (j c) -> p j c", c=32)[:, :, DEC_S * par:DEC_S * par + DEC_S]
                    own(v.tensor_copy(qi_bd[HD * par:HD * par + HD, h, :, DEC_S * par:DEC_S * par + DEC_S], src))
            own.settle()
            dve.sem_inc(qibd_ready, 1)
            for n, q in enumerate((SMP, 3, 2, 1)):
                w = SKEYS if q == SMP else P * (q + 1)
                last = ("dot", q, IH - 1) if q != SMP else ("sdotn", 1)
                was_read(dve, last)
                sc = score[q][:, 0:w]
                step(v.tensor_scalar(sc, relu[n % 2][:, 0, 0:w], wis[:, q, 0:1], None, ALU.mult))
                for h in range(1, IH):
                    step(v.scalar_tensor_tensor(sc, relu[n % 2][:, h, 0:w], wis[:, q, h:h + 1], sc, ALU.mult, ALU.add))
                dve.sem_inc(relu_used, 1)
                if q == SMP:
                    step(v.tensor_tensor(sc[:, PAST:SKEYS], sc[:, PAST:SKEYS], own_batch, ALU.add))
                else:
                    step(v.memset(sc[0:CHUNK, w - CHUNK:w], OUT_OF_REACH))
            for q in (1, 2, 3, SMP):
                w = SKEYS + SPAD if q == SMP else P * (q + 1)
                sc = score[q][:, 0:w]
                for _r in range((TOPK_S + SPAD if q == SMP else TOPK_P) // 8):
                    step(v.max(top8, sc))
                    step(v.match_replace(sc, top8, sc, TAKEN))
                w = SKEYS if q == SMP else w
                own(v.tensor_scalar(mask_bias[q], sc[:, 0:w], TAKEN_BELOW, -BIG, ALU.is_gt, ALU.mult))
                own.settle()
                dve.sem_inc(mask_ready, 1)
            own(v.memset(view(O_IX + 2560 + 4096, 1024), 0.0))
            own.settle()
            for r_ in range(REP):
                for g in range(AKV):
                    dst = qa_bd[HD * g:HD * g + HD, :, HD * g + DEC_S * r_:HD * g + DEC_S * r_ + DEC_S]
                    src = featT[HD * g:HD * g + HD, r_, SEQ:TOK].rearrange("p (b q) -> p b q", b=DEC_B)
                    own(v.tensor_copy(dst, src))
            own.settle()
            dve.sem_inc(qabd_ready, 1)

            def width(u):
                return P * (A_UNITS[u][1] + 1) if u < NP_A else SKEYS

            dve.wait_ge(m9_st[0], 96)
            dve.wait_ge(m9_st[1], 96)
            dve.wait_ge(kb_st[0], 48)
            dve.wait_ge(kb_st[1], 32)
            for i in range(NA + 3):
                if i < NA:
                    sl, _k = place[("L", i)]
                    result(dve, ("L", i))
                    own(v.tensor_reduce(nmax[:, i % 4:i % 4 + 1], ps[:, 512 * sl:512 * sl + width(i)], X, ALU.max,
                                        negate=True))
                    own.settle()
                    dve.sem_inc(nmax_ready, 1)
                if 1 <= i <= NA:
                    u = i - 1
                    c = slice(u % 4, u % 4 + 1)
                    dve.wait_ge(exp_ready, u + 1)
                    step(v.reciprocal(rrec[:, c], rsum[:, c]))
                    pr = prob[u % 3][:, 0:width(u)]
                    own(v.tensor_scalar(pr, pr, rrec[:, c], None, ALU.mult))
                    own.settle()
                    dve.sem_inc(prob_ready, 1)
                if 2 <= i < NA + 2 and i % 2 == 1:
                    u = i - 2
                    w = width(u)
                    sl, _k = place[("T", u)]
                    result(dve, ("T", u))
                    if u >= 2:
                        dve.wait_ge(av_done, u - 1)
                    own(v.tensor_copy(probT[u % 2].rearrange("p c q -> p (c q)")[:, 0:w], ps[:, 512 * sl:512 * sl + w]))
                    own.settle()
                    dve.sem_inc(pT_dve, 1)
                    dve.sem_inc(free[sl], 1)
                if i >= 3 and (i - 3 == NA - 1 or a_group(i - 2) != a_group(i - 3)):
                    gi = a_group(i - 3)
                    dve.wait_ge(av_done, i - 2)
                    r = bank(place[("O", gi)][0])
                    if gi < SMP:
                        own(v.tensor_copy(oaT[:, :, P * gi:P * gi + P], r.rearrange("p (r q) -> p r q", r=REP)))
                    else:
                        b = gi - SMP
                        for g in range(AKV):
                            own(v.tensor_copy(oaT[HD * g:HD * g + HD, :, SEQ + DEC_S * b:SEQ + DEC_S * b + DEC_S],
                                              r[HD * g:HD * g + HD, HD * g:HD * g + HD].rearrange("p (r q) -> p r q", r=REP)))
                    own.settle()
                    dve.sem_inc(free[place[("O", gi)][0]], 1)
            own(v.memset(view(O_F + 4096, 1024), 0.0))
            own.settle()
            for b in range(0, DEC_B, 1):
                for hh in range(2):
                    own(v.tensor_copy(qb_bd[HD * hh:HD * hh + HD, b, :, DEC_S * hh:DEC_S * hh + DEC_S],
                                      qbT[HD * hh:HD * hh + HD, :, SEQ + DEC_S * b:SEQ + DEC_S * b + DEC_S]))
            own.settle()
            dve.sem_inc(qbbd_ready, 1)

            def b_keys(i):
                for j in (1, 3):
                    r = result(dve, ("kcT", i, j))
                    own(v.tensor_copy(kcT[i % 2][:, j, :], r))
                    own.settle()
                    dve.sem_inc(kcT_dve, 1)
                    dve.sem_inc(free[place[("kcT", i, j)][0]], 1)

            for i in range(NB + 2):
                if i == BH:
                    b_keys(i)
                if i < NB:
                    w = 1280 if i < BH else SKEYS
                    z = ps[:, 1536 * (i % 2):1536 * (i % 2) + w]
                    e = ebuf[i % 2][:, 0:w]
                    dve.wait_ge(l_ready, i + 1)
                    v.scalar_tensor_tensor(e, z, 0.0, e, ALU.max, ALU.add).then_inc(sp_ready, 1)
                if BH <= i < NB - 1:
                    b_keys(i + 1)
                u = i - 2
                if u >= 0 and (u >= BH or u % 2 == 1):
                    gi = bo_group(u)
                    dve.wait_ge(bv_done, u + 1)
                    if u >= BH:
                        dve.sem_inc(slab_used, 1)
                    r = bank(place[("bO", gi)][0])
                    if u < BH:
                        own(v.tensor_copy(obT[:, u // 2, 0:SEQ], r))
                    else:
                        b = u - BH
                        for hh in range(2):
                            own(v.tensor_copy(obT[HD * hh:HD * hh + HD, :, SEQ + DEC_S * b:SEQ + DEC_S * b + DEC_S],
                                              r[HD * hh:HD * hh + HD, 0:128].rearrange("p (j c) -> p j c", c=32)[
                                                  :, :, DEC_S * hh:DEC_S * hh + DEC_S]))
                    own.settle()
                    dve.sem_inc(free[place[("bO", gi)][0]], 1)
            for i in range(16):
                if i >= 2:
                    dve.wait_ge(merged, i - 1)
                dve.wait_ge(sg_ready, i + 1)
                for j in range(2):
                    r = result(dve, ("mg", i, 2 + j))
                    own(v.tensor_tensor(gb[i % 2][j], sg[i % 2][j], r[:, 0:320], ALU.mult))
                    own.settle()
                    dve.sem_inc(free[place[("mg", i, 2 + j)][0]], 1)
                dve.sem_inc(gb_ready, 1)
            dve.wait_ge(x1_ld, 32)
            dve.wait_ge(bc2_ld, 16 * 18)

            def residual(t):
                for n in range(2):
                    r = result(dve, ("wo", t, n))
                    own(v.tensor_tensor(gated[n], r, g1[t == SMP][:, 512 * n:512 * n + 512], ALU.mult))
                    own.settle()
                    dve.sem_inc(free[place[("wo", t, n)][0]], 1)
                    xh = x1[:, t, 512 * n:512 * n + 512]
                    step(v.tensor_tensor(xh, xh, gated[n], ALU.add))
                dve.sem_inc(x1_ready, 1)

            def second_norm(t):
                m = bc2[t == SMP]
                dve.wait_ge(sum2_ready, t + 1)
                if t == 0:
                    dve.wait_ge(merged, 16)
                step(v.reciprocal(rstd2[:, t:t + 1], rstd2[:, t:t + 1]))
                if t >= 2:
                    result(dve, ("h2T", t - 2, 1))
                    dve.wait_ge(h2_st[t % 2], 16 * (t // 2))
                step(v.scalar_tensor_tensor(h2[t % 2], x1[:, t, :], rstd2[:, t:t + 1], m[:, 1024:2048], ALU.mult, ALU.mult))
                v.tensor_tensor(h2[t % 2], h2[t % 2], m[:, 0:1024], ALU.add).then_inc(h2_ready, 1)

            def logit_rows(t):
                r = result(dve, ("lg", t))
                read(("lg", t), v.tensor_copy(R3["lg"][:, t, :], r[:, 0:NE]))

            for t in range(NT + 3):
                if t < NT:
                    residual(t)
                if 1 <= t <= NT:
                    second_norm(t - 1)
                if t >= 3:
                    logit_rows(t - 3)
            was_read(dve, ("lg", NT - 1))
            lg, aff, bi, ing, bm, oh1, oh2, pr, sb, t1, t2 = (R3[k] for k in "lg aff bi ing bm oh1 oh2 pr sb t1 t2".split())
            full3 = [P, NT, NE]
            step(v.tensor_reduce(rmx, lg, X, ALU.max))
            own(v.tensor_tensor(lg, lg, bcast(rmx, full3, 2), ALU.subtract))
            own.settle()
            dve.sem_inc(e_in, 1)
            dve.wait_ge(e_out, 100)
            step(v.tensor_reduce(rsm, aff, X, ALU.add))
            step(v.reciprocal(rrc, rsm))
            step(v.tensor_tensor(aff, aff, bcast(rrc, full3, 2), ALU.mult))
            dve.wait_ge(g2_ld, 16 * 10)
            step(v.tensor_tensor(bi, aff, bcast(brb, full3, 1), ALU.add))
            b4 = bi.rearrange("p t (g e) -> p t g e", e=EPG)
            own(v.tensor_tensor(R4["p"], b4[:, :, :, 0], b4[:, :, :, 1], ALU.max))
            own(v.tensor_tensor(R4["q"], b4[:, :, :, 0], b4[:, :, :, 1], ALU.min))
            own(v.tensor_tensor(R4["r"], b4[:, :, :, 2], b4[:, :, :, 3], ALU.max))
            own(v.tensor_tensor(R4["s"], b4[:, :, :, 2], b4[:, :, :, 3], ALU.min))
            step(v.memset(gpad, -BIG))
            own(v.tensor_tensor(R4["m1"], R4["p"], R4["r"], ALU.max))
            own(v.tensor_tensor(R4["u"], R4["p"], R4["r"], ALU.min))
            step(v.tensor_tensor(R4["v"], R4["q"], R4["s"], ALU.max))
            step(v.tensor_tensor(R4["m2"], R4["u"], R4["v"], ALU.max))
            step(v.tensor_tensor(gpad[:, :, 0:NG], R4["m1"], R4["m2"], ALU.add))
            for t in range(NT):
                own(v.max(v8[:, t, :], gpad[:, t, :]))
            own.settle()
            for t in range(NT):
                own(v.max_index(i8[:, t, :], v8[:, t, :], gpad[:, t, :]))
            own.settle()
            step(v.tensor_copy(gidx, i8[:, :, 0]))
            step(v.tensor_tensor(ing, bcast(group_e, full3, 1), bcast(gidx, full3, 2), ALU.is_equal))
            own(v.tensor_scalar(t1, ing, -1.0, BIG, ALU.add, ALU.mult))
            step(v.tensor_tensor(bm, bi, ing, ALU.mult))
            step(v.tensor_tensor(bm, bm, t1, ALU.add))
            for t in range(NT):
                own(v.max(v8b[:, t, :], bm[:, t, :]))
            own.settle()
            for t in range(NT):
                own(v.max_index(i8b[:, t, :], v8b[:, t, :], bm[:, t, :]))
            own.settle()
            step(v.tensor_copy(eidx, i8b[:, :, 0:2]))
            own(v.tensor_tensor(oh1, bcast(iota_e, full3, 1), bcast(eidx[:, :, 0], full3, 2), ALU.is_equal))
            step(v.tensor_tensor(oh2, bcast(iota_e, full3, 1), bcast(eidx[:, :, 1], full3, 2), ALU.is_equal))
            own(v.tensor_tensor(sel_b, oh1, oh2, ALU.add))
            own.settle()
            dve.sem_inc(sel_ready, 1)
            for i, oh in enumerate((oh1, oh2)):
                step(v.tensor_tensor(t2, aff, oh, ALU.mult))
                step(v.tensor_reduce(aw[i], t2, X, ALU.add))
            step(v.tensor_tensor(den, aw[0], aw[1], ALU.add))
            step(v.reciprocal(rden, den))
            for i in range(2):
                step(v.tensor_tensor(ew[i], aw[i], rden, ALU.mult))
            r = result(dve, "cnt")
            step(v.tensor_copy(cnt, r[:, 0:NE]))
            step(v.memset(nt[0], 1.0))
            for k in range(1, NT):
                step(v.scalar_tensor_tensor(nt[k % 2], cnt, float(P * k), nt[(k - 1) % 2], ALU.is_gt, ALU.add))
            njobs = nt[(NT - 1) % 2]
            step(v.tensor_copy(ends[0], njobs))
            for k, d in enumerate((1, 2, 4, 8)):
                src, dst = ends[k % 2], ends[(k + 1) % 2]
                own(v.tensor_copy(dst[:, 0:d], src[:, 0:d]))
                own(v.tensor_tensor(dst[:, d:NE], src[:, d:NE], src[:, 0:NE - d], ALU.add))
                own.settle()
            end = ends[0]
            own(v.tensor_tensor(base, end, njobs, ALU.subtract))
            step(v.tensor_tensor(cmp, bcast(end, [P, JOBS, NE], 1), bcast(iota_j, [P, JOBS, NE], 2), ALU.is_le))
            step(v.tensor_scalar(base, base, float(P), None, ALU.mult))
            step(v.tensor_reduce(ejf, cmp, X, ALU.add))
            step(v.tensor_scalar(ejf, ejf, float(NE - 1), None, ALU.min))
            own(v.tensor_copy(eji, ejf))
            step(v.tensor_scalar(prf, iota_j.rearrange("p (j a) -> p j a", a=2)[:, :, 0], end[:, NE - 1:NE], None, ALU.is_lt))
            step(v.tensor_reduce(prs, prf, X, ALU.add))
            step(v.tensor_copy(pri, prs))
            dve.sem_inc(jobs_ready, 1)
            r = result(dve, "pre")
            step(v.tensor_tensor(sb, r[:, 0:NT * NE].rearrange("p (t e) -> p t e", t=NT), bcast(base, full3, 1), ALU.add))
            for i, oh in enumerate((oh1, oh2)):
                step(v.tensor_tensor(t2, sb, oh, ALU.mult))
                step(v.tensor_reduce(slotf[:, :, i], t2, X, ALU.add))
            step(v.tensor_copy(slots, slotf))
            dve.sem_inc(slots_ready, 1)
            step(v.memset(ids[:, JOBS:JOBS + 2, :], 0))
            for p in range(2):
                dve.wait_ge(y_st[p], 16)
            for p in range(2):
                dve.sem_inc(y_dve[p], 1)
            dve.wait_ge(xT_full[0], 1)
            v.tensor_copy(hxT[0][:, 4:8, :], bank(1).rearrange("p (k q) -> p k q", k=4)).then_inc(xT_dve[0], 1)
            pairs = v.value_load(pri[0:1, 0:1], min_val=NE // 2, max_val=PAIRS)
            with dve.Fori(0, pairs) as i:
                def hold(sm, val):
                    dve.wait_ge(sm, val)
                    dve.sem_inc(held["dve"], 1)

                def turn_x(p, n):
                    hold(xT_full[p], n)
                    v.tensor_copy(hxT[p][:, 4:8, :], bank(1).rearrange("p (k q) -> p k q", k=4)).then_inc(xT_dve[p], 1)

                def hidden(p):
                    hold(sil_done[p], i + 1)
                    dve.wait_ge(up_full[p], i + 1)
                    dve.sem_inc(mw_free[3 * p + 1], 1)
                    v.tensor_tensor(hid[p], sil[p], bank(3), ALU.mult).then_inc(hid_done[p], 1)

                def turn_h(p):
                    hold(hT_full[p], i + 1)
                    v.tensor_copy(hidT[p], bank(4).rearrange("p (k q) -> p k q", k=4)).then_inc(hidT_done[p], 1)

                def down(p):
                    hold(down_full[p], i + 1)
                    hold(y_st[p], i * 16 + 16)
                    v.tensor_copy(idd[p], ids[:, bass.ds(2 * i + p, 1), 1:2].rearrange("p j a -> p (j a)")).then_inc(y_dve[p], 1)
                    v.tensor_copy(yj[p][:, 512:1024], bank(6)).then_inc(y_dve[p], 1)

                def next_ids(p):
                    hold(hx_ld[p], i * 16 + 16)
                    nxt = ids[:, bass.ds(2 * i + (2 + p), 1), 0:1].rearrange("p j a -> p (j a)")
                    v.tensor_copy(idj[p], nxt).then_inc(idj_ready[p], 1)

                next_ids(0)
                turn_x(1, i + 1)
                next_ids(1)
                hidden(0)
                turn_h(0)
                hidden(1)
                down(0)
                turn_h(1)
                turn_x(0, i + 2)
                down(1)
            for t in range(NT):
                dve.wait_ge(a_half, t + 1)
                c = yc[t]
                step(v.scalar_tensor_tensor(c, y2[t][:, 1, :], ew[1][:, t:t + 1], y2[t][:, 0, :], ALU.mult, ALU.add))
                step(v.tensor_tensor(c, c, g2[t == SMP], ALU.mult))
                v.tensor_tensor(c, c, x1[:, t, :], ALU.add).then_inc(e_out, 1)

        @block.tensor
        def _(pe):
            mm, tr = nc.tensor.matmul, nc.tensor.transpose

            def slab_wait(s):
                n = slab_no[s]
                pe.wait_ge(slab_ld[n % NSLAB], landed[n])
                return n % NSLAB

            def slot_counts(mark):
                for s_, k_ in enumerate(marks[mark]):
                    if k_:
                        pe.wait_ge(free[s_], k_)

            def turn4(dst, blocks):
                for k, b in enumerate(blocks):
                    last = tr(dst[:, P * k:P * k + P], b, ident)
                return last

            pe.wait_ge(c_ld, 32)
            pe.wait_ge(s9_ready, 1)
            b = may_fill("s9T")
            for k in range(KD):
                last = tr(b[:, NCOND * k:NCOND * (k + 1)], s9[:, P * k:P * (k + 1)], ident[0:NCOND, 0:NCOND])
            filled("s9T", last)
            pe.wait_ge(s9T_ready, 1)

            def ada(i):
                n = slab_wait(("ada", i))
                b = may_fill(("ada", i))
                for k in range(KD):
                    last = mm(b[0:NCOND], s9T[:, k, :], slab_k[n][:, k, :], start=(k == 0), stop=(k == KD - 1))
                filled(("ada", i), last)
                result(pe, ("ada", i))
                pe.sem_inc(slab_used, 1)

            for i in range(8):
                ada(i)
            for t in range(NT):
                pe.wait_ge(h_ready, t + 1)
                for h in range(2):
                    b = may_fill(("h1T", t, h))
                    filled(("h1T", t, h), turn4(b, [ht[t % 2][:, P * k:P * k + P] for k in range(4 * h, 4 * h + 4)]))

            def rows(name, w=512, after=None):
                n = slab_wait(("in", name))
                for t in range(NT):
                    if name == "qa":
                        was_read(pe, ("h1T", t, 1))
                        was_read(pe, ("h1T", t, 0))
                    b = may_fill((name, t))
                    for k in range(KD):
                        last = mm(b[:, 0:w], hT[:, k, P * t:P * t + P], slab_k[n][:, k, 0:w], start=(k == 0), stop=(k == KD - 1))
                    filled((name, t), last)
                    if after:
                        after(t)
                result(pe, (name, NT - 1))
                pe.sem_inc(slab_used, 1)

            rows("qa")
            rows("kvq")
            rows("kiwi", 68)
            n = slab_wait(("in", "qb"))
            for m in range(4):
                for h in range(2):
                    b = may_fill(("qb", m, h))
                    for k in range(KD):
                        last = mm(b[:, 0:320], slab_k[n][:, k, P * m:P * m + P], hT[:, k, 320 * h:320 * h + 320],
                                  start=(k == 0), stop=(k == KD - 1))
                    filled(("qb", m, h), last)
            result(pe, ("qb", 3, 1))
            pe.sem_inc(slab_used, 1)
            rows("vb")
            for t in range(NT):
                pe.wait_ge(ro_ready, t + 1)
                for h in range(2):
                    b = may_fill(("roT", t, h))
                    filled(("roT", t, h), turn4(b, [ro[t % 2][:, P * k:P * k + P] for k in range(4 * h, 4 * h + 4)]))
            n = slab_wait(("idx",))
            v_ = slab[n][:, 0:2048].rearrange("p (j c n) -> p j c n", j=4, c=4)
            for j in range(4):
                b = may_fill(("idxT", j))
                filled(("idxT", j), turn4(b, [v_[:, j, c, :] for c in range(4)]))
            result(pe, ("idxT", 3))
            pe.sem_inc(slab_used, 1)
            for j in range(4):
                was_read(pe, ("idxT", j))
            for t in range(NT):
                for h in range(2):
                    was_read(pe, ("roT", t, h))
            pe.wait_ge(qibd_ready, 1)
            for h in range(IH):
                b = may_fill(("sdot", h))
                for j in range(4):
                    last = mm(b[32 * j:32 * j + 32], qi_bd[:, h, j, :], idxT[:, j, :], start=True, stop=True)
                filled(("sdot", h), last)
            for par in range(2):
                b = may_fill(("sdotn", par))
                q = slice(HD * par, HD * par + HD)
                for j in range(2):
                    last = mm(b[:, P * j:P * j + P], featT[q, 5 + j, SEQ:TOK], featT[q, 7, SEQ:TOK], start=True, stop=True)
                filled(("sdotn", par), last)
            for t in (3, 2, 1):
                for h in range(IH):
                    q = slice(HD * (h % 2), HD * (h % 2) + HD)
                    b = may_fill(("dot", t, h))
                    filled(("dot", t, h), mm(b[:, 0:P * (t + 1)], featT[q, 5 + h // 2, P * t:P * t + P],
                                             featT[q, 7, 0:P * (t + 1)], start=True, stop=True))

            def turn_kb(t):
                pe.wait_ge(kbt_ready, t + 1)
                b = may_fill(("kbT", t))
                filled(("kbT", t), turn4(b, [kbt[t % 2][:, P * k:P * k + P] for k in range(NPAIR)]))

            rows("kb", after=lambda t: turn_kb(t - 1) if t else None)
            turn_kb(NT - 1)
            for i in range(8, 12):
                ada(i)
            slot_counts("a")
            nk = slab_wait(("ak",))
            nv = slab_wait(("av",))
            cak = slab[nk].rearrange("p (b c n) -> p b c n", b=DEC_B, c=4)
            cav = slab[nv].rearrange("p (b c n) -> p b c n", b=DEC_B, c=4)
            pe.wait_ge(relu_used, 4)
            for b_ in range(DEC_B):
                b = may_fill(("kaT", b_))
                filled(("kaT", b_), turn4(b, [cak[:, b_, c, :] for c in range(4)]))
            result(pe, ("kaT", DEC_B - 1))
            pe.sem_inc(slab_used, 1)
            for b_ in range(DEC_B):
                was_read(pe, ("kaT", b_))
            pe.wait_ge(mask_ready, 1)

            def logits(u):
                may_fill(("L", u))
                sl, _k = place[("L", u)]
                un = A_UNITS[u]
                if un[0] == "p":
                    _p, q, r, g = un
                    b = bank(sl)
                    w = P * (q + 1)
                    if q:
                        pe.wait_ge(mask_ready, q)
                    gs = slice(HD * g, HD * g + HD)
                    mm(b[:, 0:w], ident_b, mask_bias[q] if q else chunk_b, start=True, stop=False)
                    last = mm(b[:, 0:w], featT[gs, r, P * q:P * q + P], featT[gs, 4, 0:w], start=False, stop=True)
                else:
                    s_ = un[1]
                    if s_ < 2:
                        for w_ in range(NP_A - 3, NP_A):
                            was_read(pe, ("L", w_))
                    pe.wait_ge(mask_ready, 4)
                    pe.wait_ge(qabd_ready, 1)
                    for lo, w, keys in ((0, PAST, kaT[:, s_, :]), (PAST, P, featT[:, 4, SEQ:TOK])):
                        d = ps[:, 512 * sl + lo:512 * sl + lo + w]
                        mm(d, pick_b[:, s_, :], mask_bias[SMP][:, lo:lo + w], start=True, stop=False)
                        last = mm(d, qa_bd[:, s_, :], keys, start=False, stop=True)
                filled(("L", u), last)

            def turn_prob(u):
                may_fill(("T", u))
                sl, _k = place[("T", u)]
                if u == NP_A:
                    was_read(pe, ("T", u - 1))
                pe.wait_ge(prob_ready, u + 1)
                w = (A_UNITS[u][1] + 1) if u < NP_A else NC_KEYS + 1
                for c in range(w):
                    last = tr(ps[:, 512 * sl + P * c:512 * sl + P * c + P], prob[u % 3][:, P * c:P * c + P], ident)
                filled(("T", u), last)

            def values(u):
                gi = a_group(u)
                if u == 0 or a_group(u - 1) != gi:
                    may_fill(("O", gi))
                b = bank(place[("O", gi)][0])
                pe.wait_ge(pT_act if u % 2 == 0 else pT_dve, u // 2 + 1)
                un = A_UNITS[u]
                if un[0] == "p":
                    _p, q, r, g = un
                    for c in range(q + 1):
                        last = mm(b[HD * g:HD * g + HD, P * r:P * r + P], va[:, c, HD * g:HD * g + HD], probT[u % 2][:, c, :],
                                  start=(c == 0), stop=(c == q), skip_group_check=True)
                else:
                    for c in range(NC_KEYS + 1):
                        w = cav[:, un[1], c, :] if c < NC_KEYS else va[:, SMP, :]
                        last = mm(b[:, 0:P], w, probT[u % 2][:, c, :], start=(c == 0), stop=(c == NC_KEYS),
                                  skip_group_check=True)
                last.then_inc(av_done, 1)

            for i in range(NA + 3):
                if i < NA:
                    logits(i)
                if 2 <= i < NA + 2:
                    turn_prob(i - 2)
                if i >= 3:
                    values(i - 3)
            pe.wait_ge(av_done, NA)
            pe.sem_inc(slab_used, 1)

            slot_counts("b")
            for t in range(NT):
                was_read(pe, ("kbT", t))
            pe.wait_ge(vb_ready, NT)

            def zreg(i):
                return ps[:, 1536 * (i % 2):1536 * (i % 2) + 1536]

            def scores(i):
                if i >= 2:
                    pe.wait_ge(att_ready, i - 1)
                z = zreg(i)
                if i < BH:
                    hs = slice(HD * (i % 2), HD * (i % 2) + HD)
                    for c in (0, 1, 3, 2):
                        at, w = zcol[c], SEQ - P * c
                        mm(z[:, at:at + P], ident_b, later_b, start=(c != 3), stop=False, skip_group_check=True)
                        last = mm(z[:, at:at + P], kbT[hs, i // 2, P * c:P * c + P], qbT[hs, i // 2, P * c:P * c + P],
                                  start=False, stop=True, skip_group_check=True)
                        if w > P:
                            last = mm(z[:, at + P:at + w], kbT[hs, i // 2, P * c:P * c + P],
                                      qbT[hs, i // 2, P * c + P:SEQ], start=False, stop=True, skip_group_check=True)
                else:
                    b_ = i - BH
                    pe.wait_ge(kcT_act, 2 * b_ + 2)
                    pe.wait_ge(kcT_dve, 2 * b_ + 2)
                    pe.wait_ge(qbbd_ready, 1)
                    for c in range(NC_KEYS):
                        for j in range(NPAIR):
                            mm(z[:, P * c + 32 * j:P * c + 32 * j + 32], kcT[i % 2][:, j, P * c:P * c + P], qb_bd[:, b_, j, :],
                               start=(c == 0 and j == 0), stop=True, skip_group_check=True)
                    at = P * NC_KEYS
                    mm(z[:, at:at + P], ident_b, newmask_b[:, b_, :], start=True, stop=False, skip_group_check=True)
                    for j in range(NPAIR):
                        last = mm(z[:, at + 32 * j:at + 32 * j + 32], kbT[:, j, SEQ:TOK], qb_bd[:, b_, j, :],
                                  start=False, stop=True, skip_group_check=True)
                last.then_inc(z_full, 1)

            def cumulate(i):
                z, e = zreg(i), ebuf[i % 2]
                pe.wait_ge(sp_ready, i + 1)
                if i < BH:
                    for c in range(4):
                        at, w = zcol[c], SEQ - P * c
                        last = mm(z[:, at:at + w], neg_tri, e[:, at:at + w], start=False, stop=True, skip_group_check=True)
                        for c2 in range(c + 1, 4):
                            w2 = SEQ - P * c2
                            last = mm(z[:, at + w - w2:at + w], neg_ones, e[:, zcol[c2]:zcol[c2] + w2], start=False, stop=True,
                                      skip_group_check=True)
                else:
                    mm(z[:, 0:PAST], neg_tri, e[:, 0:PAST], start=False, stop=True, skip_group_check=True)
                    last = mm(z[:, PAST:SKEYS], neg_tri, e[:, PAST:SKEYS], start=False, stop=True, skip_group_check=True)
                    for c2 in range(1, NC_KEYS + 1):
                        last = mm(z[:, 0:P * c2].rearrange("p (c q) -> p c q", q=P), neg_ones,
                                  bcast(e[:, P * c2:P * c2 + P], [P, c2, P], 1), start=False, stop=True, skip_group_check=True)
                last.then_inc(cum_full, 1)

            def b_values(i):
                gi = bo_group(i)
                if i >= BH or i % 2 == 0:
                    may_fill(("bO", gi))
                b = bank(place[("bO", gi)][0])
                pe.wait_ge(att_ready, i + 1)
                if i < BH:
                    hs = slice(HD * (i % 2), HD * (i % 2) + HD)
                    for c in range(4):
                        at, w = zcol[c], SEQ - P * c
                        last = mm(b[hs, P * c:SEQ], vb[:, c, HD * i:HD * i + HD], att[i % 2][:, at:at + w],
                                  start=(c == 0), stop=(c == 3), skip_group_check=True)
                else:
                    b_ = i - BH
                    cbv = slab[slab_no[("b", b_)] % NSLAB].rearrange("p (w c n) -> p w c n", w=2, c=4)[:, 1]
                    for j in range(NPAIR):
                        for c in range(NC_KEYS + 1):
                            w = cbv[:, c, P * j:P * j + P] if c < NC_KEYS else vb[:, SMP, P * j:P * j + P]
                            last = mm(b[:, 32 * j:32 * j + 32], w, att[i % 2][:, P * c + 32 * j:P * c + 32 * j + 32],
                                      start=(c == 0), stop=(c == NC_KEYS), skip_group_check=True)
                last.then_inc(bv_done, 1)

            def turn_keys(i):
                n = slab_wait(("b", i - BH))
                cbk = slab[n].rearrange("p (w c n) -> p w c n", w=2, c=4)[:, 0]
                for j in range(NPAIR):
                    b = may_fill(("kcT", i, j))
                    filled(("kcT", i, j), turn4(b, [cbk[:, c, P * j:P * j + P] for c in range(4)]))

            for i in range(NB + 2):
                if i == BH:
                    cumulate(i - 1)
                    pe.wait_ge(att_ready, BH)
                    turn_keys(i)
                if i < NB:
                    scores(i)
                if BH <= i < NB - 1:
                    turn_keys(i + 1)
                if 1 <= i <= NB and i != BH:
                    cumulate(i - 1)
                if i >= 2:
                    b_values(i - 2)
            slot_counts("m")
            pe.wait_ge(att_ready, NB)
            for i in range(16):
                m, h = i // 2, i % 2
                hc = slice(320 * h, 320 * h + 320)
                for j in range(4):
                    if j < 2:
                        if i < 8:
                            w = slab_k[slab_no[("gl", j, 0)] % NSLAB]
                            if i == 0:
                                slab_wait(("gl", j, 0))
                        else:
                            w = gx[j]
                            if i == 8:
                                pe.wait_ge(gx_ld[j], 16)
                        rhs, kk, col = hT, KD, m % 4
                    else:
                        branch = (("bra",), ("brb",))[j - 2]
                        if i == 0:
                            slab_wait(branch)
                        w, rhs, kk, col = slab_4[slab_no[branch] % NSLAB], (oaT, obT)[j - 2], 4, m
                    b = may_fill(("mg", i, j))
                    for k in range(kk):
                        last = mm(b[:, 0:320], w[:, k, P * col:P * col + P], rhs[:, k, hc], start=(k == 0), stop=(k == kk - 1))
                    filled(("mg", i, j), last)
                if i == 7:
                    result(pe, ("mg", i, 3))
                    pe.sem_inc(slab_used, 2)
            result(pe, ("mg", 15, 3))
            pe.sem_inc(merge_read, 2)
            slot_counts("o")
            pe.wait_ge(merged, 16)
            n0, n1 = slab_wait(("wo", 0)), slab_wait(("wo", 1))

            def turn_h2(t):
                pe.wait_ge(h2_ready, t + 1)
                for h in range(2):
                    b = may_fill(("h2T", t, h))
                    filled(("h2T", t, h), turn4(b, [h2[t % 2][:, P * k:P * k + P] for k in range(4 * h, 4 * h + 4)]))

            def router_logits(t):
                pe.wait_ge(h2T_ready, t + 1)
                b = may_fill(("lg", t))
                for k in range(KD):
                    last = mm(b[:, 0:NE], h2T[t % 2][:, k, :], wr[:, k, :], start=(k == 0), stop=(k == KD - 1))
                filled(("lg", t), last)

            for t in range(NT + 3):
                if t < NT:
                    for n_, sn in enumerate((n0, n1)):
                        b = may_fill(("wo", t, n_))
                        for k in range(KD):
                            last = mm(b, mergedT[:, k, P * t:P * t + P], slab_k[sn][:, k, :], start=(k == 0), stop=(k == KD - 1))
                        filled(("wo", t, n_), last)
                if 2 <= t < NT + 2:
                    turn_h2(t - 2)
                if t == NT - 1:
                    result(pe, ("wo", NT - 1, 1))
                    pe.sem_inc(wo_done, 1)
                if t >= 3:
                    if t == 3:
                        pe.wait_ge(wr_ld, 16)
                    router_logits(t - 3)
            pe.wait_ge(sel_ready, 1)
            b = may_fill("pre")
            mm(b[:, 0:NT * NE], before_b, sel_b, start=True, stop=False, skip_group_check=True)
            for t in range(NT - 1):
                k = NT - 1 - t
                last = mm(b[:, NE * (t + 1):NT * NE].rearrange("p (t e) -> p t e", e=NE), ones_b,
                          bcast(sel_b[:, t, :], [P, k, NE], 1), start=False, stop=(t == NT - 2), skip_group_check=True)
            filled("pre", last)
            b = may_fill("cnt")
            for t in range(NT):
                last = mm(b[:, 0:NE], ones_b, sel_b[:, t, :], start=(t == 0), stop=(t == NT - 1))
            filled("cnt", last)
            pe.wait_ge(slots_ready, 1)
            pe.wait_ge(jobs_ready, 1)
            pairs = nc.tensor.value_load(pri[0:1, 0:1], min_val=NE // 2, max_val=PAIRS)
            pe.wait_ge(hx_ld[0], 16)
            turn4(bank(0), [hx[0][:, P * k:P * k + P] for k in range(4)])
            turn4(bank(1), [hx[0][:, P * k:P * k + P] for k in range(4, 8)]).then_inc(xT_full[0], 1)
            with pe.Fori(0, pairs) as i:
                def hold(sm, v):
                    pe.wait_ge(sm, v)
                    pe.sem_inc(held["pe"], 1)

                def turn_x(p, n):
                    hold(hx_ld[p], n * 16)
                    turn4(bank(0), [hx[p][:, P * k:P * k + P] for k in range(4)])
                    turn4(bank(1), [hx[p][:, P * k:P * k + P] for k in range(4, 8)]).then_inc(xT_full[p], 1)

                def project(p, w, b, done):
                    hold(mw_ld[3 * p + w], i * 16 + 16)
                    wk = mw[3 * p + w].rearrange("p (k n) -> p k n", k=KD)
                    for k in range(KD):
                        last = mm(bank(b), hxT[p][:, k, :], wk[:, k, :], start=(k == 0), stop=(k == KD - 1))
                    last.then_inc(done, 1)

                def gate(p):
                    hold(xT_act[p], i + 1)
                    hold(xT_dve[p], i + 1)
                    if p:
                        hold(sil_done[0], i + 1)
                    project(p, 0, 2, gate_full[p])

                def turn_h(p):
                    hold(hid_done[p], i + 1)
                    turn4(bank(4), [hid[p][:, P * k:P * k + P] for k in range(4)]).then_inc(hT_full[p], 1)

                def down(p):
                    hold(hidT_done[p], i + 1)
                    hold(mw_ld[3 * p + 2], i * 16 + 16)
                    if p:
                        hold(y_act[0], i + 2)
                        hold(y_dve[0], 2 * i + 3)
                    else:
                        hold(y_act[1], i + 1)
                        hold(y_dve[1], 2 * i + 1)
                    wk = mw[3 * p + 2].rearrange("p (k n) -> p k n", k=4)
                    for h in range(2):
                        for k in range(4):
                            last = mm(bank(5 + h), hidT[p][:, k, :], wk[:, k, 512 * h:512 * h + 512], start=(k == 0), stop=(k == 3))
                    last.then_inc(down_full[p], 1)

                gate(0)
                turn_x(1, i + 1)
                project(0, 1, 3, up_full[0])
                gate(1)
                turn_h(0)
                project(1, 1, 3, up_full[1])
                down(0)
                turn_h(1)
                turn_x(0, i + 2)
                down(1)


_INS = ["x_prompt", "x_sample", "cache_a_k", "cache_a_v", "cache_idx_k", "cache_b_k", "cache_b_v", "c_prompt", "c_sample",
        "norm1_g", "norm2_g", "w_ada", "b_ada", "w_in", "qn_g", "kn_g", "w_branch_a", "w_branch_b", "w_out", "w_router",
        "b_router", "w_exp_gate", "w_exp_up", "w_exp_down"]


def _out_shapes():
    p, s = (1, 1, SEQ), (1, DEC_B, DEC_S)
    shapes = [(1, SEQ, D), (DEC_B, DEC_S, D)]
    for lead in (p, s):
        shapes += [lead + (AKV, HD), lead + (AKV, HD), lead + (HD,), lead + (BH, HD), lead + (BH, HD)]
    return shapes


def kernel(**inputs):
    import concourse.bacc as bacc
    from concourse.bass_utils import run_bass_kernel_spmd

    nc = bacc.Bacc("TRN2", target_bir_lowering=False, num_devices=1)
    arrays, a = {}, {}
    given = {n: np.ascontiguousarray(inputs[n]) for n in _INS}
    given.update(host_constants())
    for name, arr in given.items():
        arrays[f"in_{name}"] = arr
        a[name] = nc.dram_tensor(f"in_{name}", arr.shape, mybir.dt.from_np(arr.dtype), kind="ExternalInput").ap()
    shapes = _out_shapes()
    outs = [nc.dram_tensor(f"out_{i}", s, F32, kind="ExternalOutput").ap() for i, s in enumerate(shapes)]
    scratch = (nc.dram_tensor("mod_rows", (NCOND, 6 * D), F32).ap(), nc.dram_tensor("h2_rows", (TOK, D), F32).ap(),
               nc.dram_tensor("expert_rows", (2 * TOK + JOBS * P, D), F32).ap(), nc.dram_tensor("slot_tokens", (JOBS * P, 2), I32).ap())
    build(nc, a, outs, scratch)
    r = run_bass_kernel_spmd(nc, [arrays], core_ids=[0])
    return tuple(r.results[0][f"out_{i}"] for i in range(len(shapes)))
```
